# Optimizing a Trainium2 kernel written in Bass

```python
import jax, jax.numpy as jnp
from jax import lax
import numpy as np

D_MODEL = 1024
BATCH = 1
SEQ = 512
DEPTH = 2

GRID_W = 64
CTX_LEN = 256
N_MIXERS = 2
N_HEADS = 16
HEAD_DIM = D_MODEL // N_HEADS
WIN_ROWS = 8
WIN_COLS = 16
CONV_WIDTH = 3
MLP_MULT = 4
D_FF = MLP_MULT * D_MODEL
N_CONV_LAYERS = (DEPTH + 1) // 2
N_ATTN_LAYERS = DEPTH // 2
RMS_EPS = 1e-6
NEG_INF = -1e30
ATTN_SCALE = HEAD_DIM ** -0.5

kernel_name = "hybrid_conv_natten_dit_block"

def rmsnorm(x, g):
    xf = x.astype(jnp.float32)
    inv = lax.rsqrt(jnp.mean(xf * xf, axis=-1, keepdims=True) + RMS_EPS)
    return (xf * inv).astype(x.dtype) * g

def ada_terms(cond, w, b):
    m = jax.nn.silu(cond) @ w + b
    return jnp.split(m[..., None, :], 6, axis=-1)

def modulate(h, shift, scale):
    return h * (1.0 + scale) + shift

def squared_relu_mlp(h, w1, w2):
    return jnp.square(jax.nn.relu(h @ w1)) @ w2

def depthwise_conv_centred(u, w):
    pad = CONV_WIDTH // 2
    L = u.shape[1]
    up = jnp.pad(u, ((0, 0), (pad, pad), (0, 0)))
    out = up[:, 0:L] * w[0]
    for j in range(1, CONV_WIDTH):
        out = out + up[:, j:j + L] * w[j]
    return out

def short_conv_mixer(h, w_in, w_conv, w_out):
    b_gate, c_gate, v = jnp.split(h @ w_in, 3, axis=-1)
    return (b_gate * depthwise_conv_centred(c_gate * v, w_conv)) @ w_out

def split_heads(t):
    B, L, _ = t.shape
    return t.reshape(B, L, N_HEADS, HEAD_DIM).transpose(0, 2, 1, 3)

def merge_heads(t):
    B, H, L, dh = t.shape
    return t.transpose(0, 2, 1, 3).reshape(B, L, H * dh)

def dense_ctx_attention(qc, kc, vc):
    s = jnp.einsum('bhqd,bhkd->bhqk', qc, kc).astype(jnp.float32) * ATTN_SCALE
    p = jax.nn.softmax(s, axis=-1).astype(vc.dtype)
    return jnp.einsum('bhqk,bhkd->bhqd', p, vc)

def neighbourhood_latent_attention(q, k, v, kc, vc, rpb):
    B, H, S, dh = q.shape
    rows = S // GRID_W
    kh = min(WIN_ROWS, rows)
    q = q.reshape(B, H, rows, GRID_W, dh) * ATTN_SCALE
    k = k.reshape(B, H, rows, GRID_W, dh)
    v = v.reshape(B, H, rows, GRID_W, dh)

    cols = jnp.arange(GRID_W)
    col_start = jnp.clip(cols - WIN_COLS // 2, 0, GRID_W - WIN_COLS)
    col_mask = (cols[None, :] >= col_start[:, None]) & (cols[None, :] < col_start[:, None] + WIN_COLS)
    dc = jnp.clip(cols[None, :] - cols[:, None] + (WIN_COLS - 1), 0, 2 * WIN_COLS - 2)

    def one_row(r):
        rs = jnp.clip(r - kh // 2, 0, rows - kh)
        q_r = lax.dynamic_index_in_dim(q, r, axis=2, keepdims=False)
        k_rb = lax.dynamic_slice_in_dim(k, rs, kh, axis=2)
        v_rb = lax.dynamic_slice_in_dim(v, rs, kh, axis=2)
        dr = rs + jnp.arange(kh) - r + (WIN_ROWS - 1)
        bias = rpb[:, dr[:, None, None], dc[None, :, :]].transpose(0, 2, 1, 3)
        s_loc = jnp.einsum('bhqd,bhrkd->bhqrk', q_r, k_rb).astype(jnp.float32) + bias.astype(jnp.float32)
        s_loc = jnp.where(col_mask[None, None, :, None, :], s_loc, NEG_INF)
        s_ctx = jnp.einsum('bhqd,bhkd->bhqk', q_r, kc).astype(jnp.float32)
        s_all = jnp.concatenate([s_loc.reshape(B, H, GRID_W, kh * GRID_W), s_ctx], axis=-1)
        p = jax.nn.softmax(s_all, axis=-1).astype(v.dtype)
        p_loc = p[..., :kh * GRID_W].reshape(B, H, GRID_W, kh, GRID_W)
        p_ctx = p[..., kh * GRID_W:]
        return (jnp.einsum('bhqrk,bhrkd->bhqd', p_loc, v_rb)
                + jnp.einsum('bhqk,bhkd->bhqd', p_ctx, vc))

    out = lax.map(one_row, jnp.arange(rows))
    return out.transpose(1, 0, 3, 2, 4).reshape(B, S, H * dh)

def neighbourhood_attention_mixer(h, hc, w_qkv, rpb, w_out, with_ctx_queries):
    D = h.shape[-1]
    q, k, v = [split_heads(t) for t in jnp.split(h @ w_qkv, 3, axis=-1)]
    if with_ctx_queries:
        qc, kc, vc = [split_heads(t) for t in jnp.split(hc @ w_qkv, 3, axis=-1)]
    else:
        kc, vc = [split_heads(t) for t in jnp.split(hc @ w_qkv[:, D:], 2, axis=-1)]
    y = neighbourhood_latent_attention(q, k, v, kc, vc, rpb) @ w_out
    yc = merge_heads(dense_ctx_attention(qc, kc, vc)) @ w_out if with_ctx_queries else None
    return y, yc

def setup_inputs(seed: int = 0) -> dict:
    key = jax.random.key(seed)
    ks = jax.random.split(key, 17)
    D = D_MODEL

    def nrm(k, shape, s):
        return jax.random.normal(k, shape, jnp.float32) * s

    return {
        "x": nrm(ks[0], (BATCH, SEQ, D), 1.0),
        "c": nrm(ks[1], (BATCH, D), 1.0),
        "ctx": nrm(ks[2], (BATCH, CTX_LEN, D), 1.0),
        "c_ctx": nrm(ks[3], (D,), 1.0),
        "norm1_g": 1.0 + nrm(ks[4], (DEPTH, D), 0.02),
        "norm2_g": 1.0 + nrm(ks[5], (DEPTH, D), 0.02),
        "ada_w": nrm(ks[6], (DEPTH, D, 6 * D), D ** -0.5),
        "ada_b": nrm(ks[7], (DEPTH, 6 * D), 0.01),
        "conv_in_w": nrm(ks[8], (N_CONV_LAYERS, D, 3 * D), D ** -0.5),
        "conv_w": nrm(ks[9], (N_CONV_LAYERS, CONV_WIDTH, D), CONV_WIDTH ** -0.5),
        "conv_out_w": nrm(ks[10], (N_CONV_LAYERS, D, D), D ** -0.5),
        "attn_qkv_w": nrm(ks[11], (N_ATTN_LAYERS, D, 3 * D), D ** -0.5),
        "attn_rpb": nrm(ks[12], (N_ATTN_LAYERS, N_HEADS, 2 * WIN_ROWS - 1, 2 * WIN_COLS - 1), 0.1),
        "attn_out_w": nrm(ks[13], (N_ATTN_LAYERS, D, D), D ** -0.5),
        "mlp_w1": nrm(ks[14], (DEPTH, D, D_FF), D ** -0.5),
        "mlp_w2": nrm(ks[15], (DEPTH, D_FF, D), D_FF ** -0.5),
        "final_g": 1.0 + nrm(ks[16], (D,), 0.02),
    }

def reference(x, c, ctx, c_ctx, norm1_g, norm2_g, ada_w, ada_b, conv_in_w, conv_w, conv_out_w,
              attn_qkv_w, attn_rpb, attn_out_w, mlp_w1, mlp_w2, final_g):
    for i in range(DEPTH):
        last = i == DEPTH - 1
        j = i // N_MIXERS
        sh1, sc1, gt1, sh2, sc2, gt2 = ada_terms(c, ada_w[i], ada_b[i])
        csh1, csc1, cgt1, csh2, csc2, cgt2 = ada_terms(c_ctx, ada_w[i], ada_b[i])
        h = modulate(rmsnorm(x, norm1_g[i]), sh1, sc1)
        if i % N_MIXERS == 0:
            y = short_conv_mixer(h, conv_in_w[j], conv_w[j], conv_out_w[j])
            if not last:
                hc = modulate(rmsnorm(ctx, norm1_g[i]), csh1, csc1)
                yc = short_conv_mixer(hc, conv_in_w[j], conv_w[j], conv_out_w[j])
        else:
            hc = modulate(rmsnorm(ctx, norm1_g[i]), csh1, csc1)
            y, yc = neighbourhood_attention_mixer(h, hc, attn_qkv_w[j], attn_rpb[j], attn_out_w[j],
                                                  with_ctx_queries=not last)
        x = x + gt1 * y
        x = x + gt2 * squared_relu_mlp(modulate(rmsnorm(x, norm2_g[i]), sh2, sc2), mlp_w1[i], mlp_w2[i])
        if not last:
            ctx = ctx + cgt1 * yc
            ctx = ctx + cgt2 * squared_relu_mlp(modulate(rmsnorm(ctx, norm2_g[i]), csh2, csc2),
                                                mlp_w1[i], mlp_w2[i])
    return rmsnorm(x, final_g)


_drawn_inputs = setup_inputs


def setup_inputs(seed=0):
    import zlib

    import numpy as np

    out = dict(_drawn_inputs(seed))
    spreads = {}
    factors = {'norm2_g': 3.351, 'attn_rpb': 64.0, 'final_g': 23.506, 'ctx': 64.0, 'c_ctx': 8.0}
    for name, (base, spread) in spreads.items():
        noise = np.random.default_rng([zlib.crc32(name.encode()), seed]).standard_normal(out[name].shape)
        drawn = base * np.exp(spread * noise) if base else spread * noise
        out[name] = __import__('jax').numpy.asarray(drawn.astype(out[name].dtype))
    for name, factor in factors.items():
        out[name] = (out[name] * factor).astype(out[name].dtype)
    return out
```

```python
from contextlib import ExitStack

import numpy as np

import concourse.bass as bass
from concourse import mybir

F32 = mybir.dt.float32
F32R = mybir.dt.float32r
ALU = mybir.AluOpType
ACT = mybir.ActivationFunctionType
AX_X = mybir.AxisListType.X

P = 128
D = 1024
KT = D // P
LAT, CTX = 512, 256
TOK = LAT + CTX
ROWS, COLS = 8, 64
HEADS, DH = 16, 64
WIN = 16
F = 4 * D
CHUNKS = F // D
EPS = 1e-6
MASKED = -1e30
LOWEST = -3.0e38
ATTN_SCALE = DH ** -0.5

U_CONV_IN = 0
U_CONV_OUT = U_CONV_IN + 3 * KT
U_MLP = [U_CONV_OUT + KT, 0]
U_ATTN = U_MLP[0] + 2 * KT * CHUNKS
U_ATTN_OUT = U_ATTN + 3 * KT
U_MLP[1] = U_ATTN_OUT + KT
UNITS = U_MLP[1] + 2 * KT * CHUNKS
PRO = KT

WIDTH = [24, 32, 32, 24]
KEYS = [[(0, 64), (128, 256)], [(128, 384)], [(256, 512)], [(384, 512), (64, 128)]]
KEY_TILES = [
    [(0, 0, 64, 0), (1, 0, 128, 64)],
    [(1, 0, 128, 0), (2, 0, 128, 128)],
    [(2, 0, 128, 0), (3, 0, 128, 128)],
    [(3, 0, 128, 0), (0, 64, 128, 64)],
]
Q_ORDER = [(0, 64, 0), (128, 512, 64), (64, 128, 448)]
MASK_OF = [0, 1, 1, 2]
GROUPS, GH = 4, 4
BPITCH = 47
BHEAD = 15 * BPITCH + 15
BRUN = ROWS * BPITCH


def constants():
    ident = np.eye(P, dtype=np.float32)
    sel = np.zeros((P, P), np.float32)
    mask = np.zeros((P, 3, 32), np.float32)
    for half in (0, 64):
        for qc in range(WIN):
            sel[half + qc, qc * ROWS:(qc + 1) * ROWS] = 1.0
            for m, start in enumerate((max(qc - 8, 0), qc, min(qc, 8))):
                mask[half + qc, m, :] = MASKED
                mask[half + qc, m, start:start + WIN] = 0.0
    return np.ascontiguousarray(np.concatenate([ident, sel, mask.reshape(P, 96)], axis=1))


NCONST = 2 * P + 96


def free(view, dims):
    return bass.AP(view.tensor, view.offset, [list(view.ap[0])] + dims)


def build(nc, x, c, ctx, c_ctx, norm1_g, norm2_g, ada_w, ada_b, conv_in_w, conv_w, conv_out_w,
          attn_qkv_w, attn_rpb, attn_out_w, mlp_w1, mlp_w2, final_g, consts, out):
    base = (nc.sbuf_base + 63) // 64 * 64

    def at(name, shape, dt, word):
        assert base + 4 * (word + int(np.prod(shape[1:]))) <= nc.sbuf_usable_end, name
        return nc.alloc_sbuf_tensor_at(name, shape, dt, offset=base + 4 * word)

    o_x = 0
    o_h = o_x + KT * TOK
    o_g = o_h + 2 * KT * TOK
    o_s = o_g + 2 * KT * TOK
    o_wr = o_s + 6400
    o_ar = o_wr + 2 * KT * P
    o_wh = o_ar + 2 * KT * P
    o_wl = o_wh + 4 * KT * P
    o_acc = o_wl + 4 * KT * P
    o_misc = o_acc + 2 * 2 * 512

    XL = at("x_latent", [P, KT, LAT], F32, o_x)
    XC = at("x_context", [P, KT, CTX], F32, o_x + KT * LAT)
    BT = at("bias_rows", [P, GH, BRUN], F32, o_x + KT * LAT)
    HH = at("h_hi", [P, KT, TOK], F32R, o_h)
    HL = at("h_lo", [P, KT, TOK], F32R, o_h + KT * TOK)
    XN = at("x_rows", [P, TOK // P, D], F32, o_h)
    PRA = at("param_rows_a", [80, P], F32, o_h + KT * TOK)
    PRB = at("param_rows_b", [96, P], F32, o_h + KT * TOK + P)
    RPB = at("rpb_reversed", [HEADS, BHEAD], F32, o_h + KT * TOK + 2 * P)
    RPN = at("rpb_rows", [HEADS, 15, 31], F32, o_h + KT * TOK + 2 * P + BHEAD)
    OUTB = at("out_rows", [P, KT, LAT // P, P], F32, o_h)
    GH_ = at("g_hi", [P, KT, TOK], F32R, o_g)
    GL_ = at("g_lo", [P, KT, TOK], F32R, o_g + KT * TOK)
    ADAF = at("ada_first", [P, KT, 2 * D], F32, o_g)
    OH = at("o_hi", [P, KT, LAT], F32R, o_g)
    OL = at("o_lo", [P, KT, LAT], F32R, o_g + KT * LAT)
    QH = at("q_hi", [P, 2, LAT], F32R, o_g + 2 * KT * LAT)
    QL = at("q_lo", [P, 2, LAT], F32R, o_g + 2 * KT * LAT + 2 * LAT)
    PTH = at("pt_hi", [P, 4, 2 * P], F32R, o_g + 2 * KT * LAT + 4 * LAT)
    PTL = at("pt_lo", [P, 4, 2 * P], F32R, o_g + 2 * KT * LAT + 4 * LAT + 8 * P)
    KH = at("k_hi", [P, 2, TOK], F32R, o_s)
    KL = at("k_lo", [P, 2, TOK], F32R, o_s + 2 * TOK)
    VH = at("v_hi", [P, 6, 2 * P], F32R, o_s + 4 * TOK)
    VL = at("v_lo", [P, 6, 2 * P], F32R, o_s + 4 * TOK + 12 * P)
    CS_ = at("conv_c", [P, 2, TOK], F32, o_s)
    UU = at("conv_u", [P, 2, TOK + 8], F32, o_s + 2 * TOK)
    YY = at("conv_y", [P, 2, TOK + 8], F32, o_s + 4 * TOK + 16)
    GF = at("conv_g", [P, 2, TOK], F32, o_s + 6 * TOK + 32)
    RR = at("relu", [P, 2, TOK], F32, o_s)
    AA = at("relu2", [P, 2, TOK], F32, o_s + 2 * TOK)
    T1 = at("normed", [P, 2, TOK], F32, o_s)
    HF = at("modulated", [P, 2, TOK], F32, o_s + 2 * TOK)
    SQ = at("squares", [P, 2, TOK], F32, o_s + 4096)
    SS = at("square_sums", [P, TOK], F32, o_s + 4096 + 2 * TOK)
    WR = at("w_raw", [P, 2, KT, P], F32, o_wr)
    AR = at("ada_raw", [P, 2, 2, 512], F32, o_ar)
    WH = at("w_hi", [P, 4, KT, P], F32R, o_wh)
    WL = at("w_lo", [P, 4, KT, P], F32R, o_wl)
    AC = at("ada_acc", [P, 2, 2, 512], F32, o_acc)
    DI = at("inv_diag", [P, TOK // P, P], F32, o_acc)
    EE = at("probs", [P, 2, 2, 512], F32, o_acc)
    w = o_misc
    CO = at("consts", [P, NCONST], F32, w)
    w += NCONST
    SELR = at("selector", [P, P], F32R, w)
    w += P
    MSKR = at("window_masks", [P, 3, 32], F32R, w)
    w += 96
    ONES = at("ones", [P, P], F32, w)
    w += P
    PT_ = at("params", [P, 176], F32, w)
    w += 176
    ADA = at("ada", [P, 2, 2, 48], F32, w)
    w += 192
    AM = at("scale_terms", [P, 4, 2, KT], F32, w)
    w += 64
    CSI = at("silu_c", [P, KT, 2], F32, w)
    w += 16
    CT = at("silu_tmp", [P, 3, 16], F32, w)
    w += 48
    ST = at("stats", [P, 4, 8], F32, w)
    w += 32
    SM = at("softmax_small", [P, 2, 5, 2], F32, w)
    IDN = CO[:, 0:P]

    scratch = nc.dram_tensor("rpb_scratch", (HEADS, BHEAD), F32).ap()

    bias_rows = nc.dram_tensor("bias_rows_dram", (P, HEADS, BRUN), F32).ap()

    with ExitStack() as es:
        PS = es.enter_context(nc.psum_tensor("ps", [P, 4, 1024], F32))
        PSB = PS[:, :, :].rearrange("p s (b n) -> p (s b) n", b=2)

        def sem(name):
            return es.enter_context(nc.semaphore(name))

        x_in = [sem(f"x_in{t}") for t in range(TOK // P)]
        pa_in, pb_in, const_in, rpb_in, scratch_in = map(sem, ("pa_in", "pb_in", "const_in", "rpb_in", "scratch_in"))
        af_in = [sem(f"ada_first_in{k}") for k in range(KT)]
        w_in = [sem(f"w_in{s}") for s in range(2)]
        a_in = [sem(f"ada_in{s}") for s in range(2)]
        rows_in, bias_in, out_done = map(sem, ("rows_in", "bias_in", "out_done"))
        ones_set, rpb_zero, rpb_rev, par_t, sel_set, silu_e, silu_d, silu_r, silu_done = map(sem, (
            "ones_set", "rpb_zero", "rpb_rev", "par_t", "sel_set", "silu_e", "silu_d", "silu_r", "silu_done"))
        hi_done, lo_done, units_done, act_evac, dve_evac = map(sem, (
            "hi_done", "lo_done", "units_done", "act_evac", "dve_evac"))
        ada_used, ada_red, ada_step, ada_set, am_set = map(sem, (
            "ada_used", "ada_red", "ada_step", "ada_set", "am_set"))
        sq_done, ss_done, ms_done, var_done, sd_done, rs_done, d_done, inv_done = map(sem, (
            "sq_done", "ss_done", "ms_done", "var_done", "sd_done", "rs_done", "d_done", "inv_done"))
        t1_done, hf_ctx, hf_lat, h_hi, h_done = map(sem, ("t1_done", "hf_ctx", "hf_lat", "h_hi", "h_done"))
        y_done, y_mid, g_hi, g_done, a_done = map(sem, ("y_done", "y_mid", "g_hi", "g_done", "a_done"))
        qk_hi, v_mm, v_hi, qkv_done = map(sem, ("qk_hi", "v_mm", "v_hi", "qkv_done"))
        s_mm, m_ctx, m_all, m_neg, e_done, r_done, p_done, pt_mm, pt_hi, pt_done, o_mm, o_hi, o_done = map(sem, (
            "s_mm", "m_ctx", "m_all", "m_neg", "e_done", "r_done", "p_done", "pt_mm", "pt_hi", "pt_done",
            "o_mm", "o_hi", "o_done"))
        y_out, yt_mm, row_done = map(sem, ("y_out", "yt_mm", "row_done"))

        block = es.enter_context(nc.Block())

        SEG = {TOK: [(0, LAT), (LAT, TOK)], LAT: [(0, LAT)]}

        def evac_counts(phase, i, s):
            if phase == "conv_in":
                return 2 + i * 4 + (s + 2) // 3, PRO + i * 8 + (s - (s + 2) // 3)
            if phase == "conv_out":
                n = min(s, 0)
                return 2 + KT + (n + 2) // 3, PRO + 2 * KT + s - (n + 2) // 3
            a, d = {"mlp0": (2 + KT, PRO + 3 * KT), "mlp1": (2 + KT + CHUNKS * KT, PRO + (4 + CHUNKS) * KT),
                    "attn_out": (2 + KT + CHUNKS * KT, PRO + (3 + CHUNKS) * KT)}[phase]
            if phase == "attn_out":
                return a, d + s
            return a + i * KT + min(max(s, 0), KT), d + i * KT + min(s, 0) + max(s - KT, 0)

        def unit_index(phase, i, s):
            return {"conv_in": U_CONV_IN + i * 12, "conv_out": U_CONV_OUT, "mlp0": U_MLP[0] + i * 16,
                    "attn": U_ATTN + i * 12, "attn_out": U_ATTN_OUT, "mlp1": U_MLP[1] + i * 16}[phase] + s

        ADA_CONV = [[(s // 2, 2 * (s % 2) + n) for n in range(2)] for s in range(6)] + \
                   [[(3, s)] for s in range(4)] + [[], []]
        RED_CONV = {4: 0, 5: 1, 7: 2, 11: 3}
        ADA_MLP = [[(0, s)] for s in range(4)] + [[(1, s)] for s in range(4)] + [[], []] + \
                  [[(2, s)] for s in range(4)] + [[], []]
        RED_MLP = {8: 0, 9: 1, 15: 2}

        @block.sync
        def _(sp):
            for t in range(0, TOK // P, 2):
                src = x[0, t * P:(t + 1) * P, :] if t < 4 else ctx[0, (t - 4) * P:(t - 3) * P, :]
                sp.dma_start(XN[:, t, :], src).then_inc(x_in[t], 16)
            for k in range(0, KT, 2):
                sp.dma_start(ADAF[:, k, :], ada_w[0, k * P:(k + 1) * P, 0:2 * D]).then_inc(af_in[k], 16)

            def load(phase, i, s, src):
                u = unit_index(phase, i, s)
                sp.wait_ge(lo_done, u + 1)
                sp.dma_start(WR[:, s % 2, :, :], src).then_inc(w_in[s % 2], 16)

            cin = conv_in_w[0].rearrange("(k p) n -> p k n", p=P)
            with sp.Fori(1, 3) as i1:
                i = i1 - 1
                for s in range(12):
                    col = (D, 2 * D, 0)[s % 3]
                    load("conv_in", i, s, cin[:, :, bass.ds(i1 * (4 * P) + (s // 3 - 4) * P + col, P)])
            cout = conv_out_w[0].rearrange("(k p) n -> p k n", p=P)
            for s in range(KT):
                load("conv_out", 0, s, cout[:, :, s * P:(s + 1) * P])

            def mlp(layer, phase):
                w1 = mlp_w1[layer].rearrange("(k p) n -> p k n", p=P)
                w2 = mlp_w2[layer].rearrange("(k p) n -> p k n", p=P)
                with sp.Fori(0, CHUNKS) as i:
                    for s in range(KT):
                        load(phase, i, s, w1[:, :, bass.ds(i * D + s * P, P)])
                    for s in range(KT):
                        load(phase, i, KT + s, w2[:, bass.ds(i * KT, KT), s * P:(s + 1) * P])

            mlp(0, "mlp0")
            qkv = attn_qkv_w[0].rearrange("(k p) n -> p k n", p=P)
            sp.wait_ge(rows_in, 16 * ROWS)
            with sp.Fori(0, 2) as i:
                for gg in range(2):
                    for s in range(6):
                        load("attn", i, 6 * gg + s, qkv[:, :, bass.ds(i * 4 * P + (2 * gg + s % 2) * P + (s // 2) * D, P)])
                    sp.wait_ge(h_done, 3 * KT)
                    sp.wait_ge(m_neg, 16 * i + 8 * gg + 1)
                    sp.dma_start(BT[:, :, :], bias_rows[:, bass.ds(i * 2 * GH + gg * GH, GH), :]).then_inc(bias_in, 16)
            aout = attn_out_w[0].rearrange("(k p) n -> p k n", p=P)
            for s in range(KT):
                load("attn_out", 0, s, aout[:, :, s * P:(s + 1) * P])
            mlp(1, "mlp1")
            for k in range(KT):
                sp.wait_ge(row_done, k + 1)
                sp.dma_start(out[0].rearrange("(t p) n -> p t n", p=P)[:, :, k * P:(k + 1) * P],
                             OUTB[:, k, :, :]).then_inc(out_done, 16)
            sp.wait_ge(out_done, 16 * KT)

        @block.gpsimd
        def _(pool):
            pool.memset(ONES[:, :], 1.0).then_inc(ones_set, 1)
            pool.memset(RPB[:, :], 0.0).then_inc(rpb_zero, 1)
            rows = [(0, norm1_g.rearrange("l (k p) -> (l k) p", p=P)), (16, norm2_g.rearrange("l (k p) -> (l k) p", p=P)),
                    (32, final_g.rearrange("(k p) -> k p", p=P)), (40, conv_w[0].rearrange("j (k p) -> (j k) p", p=P)),
                    (64, c.rearrange("b (k p) -> (b k) p", p=P)), (72, c_ctx.rearrange("(k p) -> k p", p=P))]
            for r, src in rows:
                pool.dma_start(PRA[r:r + src.shape[0], :], src).then_inc(pa_in, 16)
            pool.dma_start(PRB[:, :], ada_b.rearrange("l (k p) -> (l k) p", p=P)).then_inc(pb_in, 16)
            pool.dma_start(RPN[:, :, :], attn_rpb[0]).then_inc(rpb_in, 16)
            pool.wait_ge(rpb_rev, 1)
            pool.dma_start(scratch, RPB[:, :]).then_inc(scratch_in, 16)
            pool.wait_ge(scratch_in, 16)
            for qr in range(ROWS):
                src = bass.AP(scratch.tensor, qr * BPITCH, [[1, WIN], [BHEAD, HEADS], [1, BRUN]])
                pool.dma_start(bias_rows.rearrange("(c r) h n -> r c h n", r=ROWS)[qr], src).then_inc(rows_in, 16)

            def ada_load(layer, entry, slot, block_, quarter):
                pool.wait_ge(ada_used, entry + 1)
                src = ada_w[layer].rearrange("(q k p) n -> p q k n", p=P, k=2)[:, quarter, :, bass.ds(block_ * 512, 512)]
                pool.dma_start(AR[:, slot, :, :], src).then_inc(a_in[slot], 16)

            with pool.Fori(0, 2) as i:
                n = 0
                for entries in ADA_CONV:
                    for b, q in entries:
                        ada_load(0, i * 16 + n, n % 2, i * 4 + 4 + b, q)
                        n += 1
            with pool.Fori(0, 4) as i:
                n = 0
                for entries in ADA_MLP:
                    for b, q in entries:
                        ada_load(1, i * 12 + 32 + n, n % 2, i * 3 + b, q)
                        n += 1
            with pool.Fori(0, 4) as i:
                for n in range(8):
                    j = n % 4
                    keys = ROWS * WIDTH[j] + CTX
                    pool.wait_ge(r_done, i * 8 + n + 2)
                    e = EE[:, n % 2, :, 0:keys]
                    pool.tensor_tensor(e, e, free(SM[:, n % 2, 4, 0:1], [[1, 2], [0, keys]]), ALU.mult)\
                        .then_inc(p_done, 1)

        @block.tensor
        def _(pe):
            def unit_mms(slot, wslots, hi, lo, tok, phase_waits=None):
                segs = SEG[tok]
                for k in range(KT):
                    if phase_waits:
                        phase_waits(k)
                    for sl, ws in zip(slot, wslots):
                        for p_, (wt, rt) in enumerate(((WH, hi), (WH, lo), (WL, hi))):
                            for a, b in segs:
                                mm = pe.matmul(PS[:, sl, a:b], wt[:, ws, k, :], rt[:, k, a:b],
                                               start=(k == 0 and p_ == 0), stop=(k == KT - 1 and p_ == 2))
                        if k == KT - 1:
                            mm.then_inc(units_done, 1)

            def wait_unit(phase, i, s):
                u = unit_index(phase, i, s)
                pe.wait_ge(lo_done, u + 3)

            def wait_slot(phase, i, s):
                a, d = evac_counts(phase, i, s - 3)
                pe.wait_ge(act_evac, a)
                pe.wait_ge(dve_evac, d)

            def reduce_ada(blocks_before, i, per_iter, b, slot, buf):
                pe.wait_ge(ada_used, (i * per_iter + (blocks_before + b + 1)) * 4 + 2)
                for cond in range(2):
                    for n in range(4):
                        mm = pe.matmul(PS[:, slot, TOK + cond * 4 + n:TOK + cond * 4 + n + 1],
                                       AC[:, buf, cond, n * P:(n + 1) * P], ONES[:, 0:1], start=True, stop=True)
                mm.then_inc(ada_red, 1)

            def norm(n, tok):
                nt = tok // P
                pe.wait_ge(ss_done, 7 * (n + 1))
                for t in range(nt):
                    mm = pe.matmul(PS[:, 2, t:t + 1], SS[:, t * P:(t + 1) * P], ONES[:, 0:1], start=True, stop=True)
                mm.then_inc(ms_done, 1)
                pe.wait_ge(d_done, n + 1)
                for a, b in SEG[tok]:
                    mm = pe.matmul(PS[:, 3, a:b], ONES[:, :], DI[:, a // P:b // P, :], start=True, stop=True)
                mm.then_inc(inv_done, 1)

            pe.wait_ge(const_in, 16)
            pe.wait_ge(pa_in, 96)
            pe.transpose(PS[:, 3, 0:80], PRA[:, :], CO[0:80, 0:80]).then_inc(par_t, 1)
            pe.wait_ge(pb_in, 16)
            pe.transpose(PS[:, 3, 512:512 + 96], PRB[:, :], CO[0:96, 0:96]).then_inc(par_t, 1)
            for k in range(KT):
                if k == 3:
                    pe.wait_ge(act_evac, 2)
                if k >= 4:
                    pe.wait_ge(dve_evac, k - 3)
                for t in range(TOK // P):
                    if k == 0:
                        pe.wait_ge(x_in[t], 16)
                    mm = pe.transpose(PS[:, k % 4, t * P:(t + 1) * P], XN[:, t, k * P:(k + 1) * P], IDN)
                mm.then_inc(units_done, 1)
            pe.wait_ge(ones_set, 1)
            norm(0, TOK)
            pe.wait_ge(silu_done, 1)
            for k in range(KT):
                pe.wait_ge(af_in[k], 16)
                for n in range(16):
                    mm = pe.matmul(PS[:, 0, 2 * n:2 * n + 2], ADAF[:, k, n * P:(n + 1) * P], CSI[:, k, :],
                                   start=(k == 0 and n == 0), stop=(k == KT - 1), skip_group_check=True)
                    if k == KT - 1 and n % 8 == 7:
                        mm.then_inc(ada_red, 1)

            with pe.Fori(0, 2) as i:
                for s in range(12):
                    if s == 1:
                        continue
                    if s in RED_CONV:
                        wait_slot("conv_in", i, s)
                        reduce_ada(0, i, 4, RED_CONV[s], s % 4, RED_CONV[s] % 2)
                    if s == 0:
                        wait_unit("conv_in", i, 1)
                        wait_slot("conv_in", i, 1)
                        unit_mms([0, 1], [0, 1], HH, HL, TOK, lambda k: pe.wait_ge(h_done, k + 1))
                    else:
                        wait_unit("conv_in", i, s)
                        wait_slot("conv_in", i, s)
                        unit_mms([s % 4], [s % 4], HH, HL, TOK)
            for s in range(KT):
                wait_unit("conv_out", 0, s)
                wait_slot("conv_out", 0, s)
                unit_mms([s % 4], [s % 4], GH_, GL_, TOK, (lambda k: pe.wait_ge(g_done, k + 1)) if s == 0 else None)
            norm(1, TOK)

            def mlp(layer, phase, tok, norm_no):
                with pe.Fori(0, CHUNKS) as i:
                    for s in range(2 * KT):
                        if s == 1:
                            continue
                        if layer == 0 and s in RED_MLP:
                            wait_slot(phase, i, s)
                            reduce_ada(8, i, 3, RED_MLP[s], s % 4, RED_MLP[s] % 2)
                        if s == 0:
                            wait_unit(phase, i, 1)
                            wait_slot(phase, i, 1)
                            unit_mms([0, 1], [0, 1], HH, HL, tok, lambda k: pe.wait_ge(h_done, norm_no * KT + k + 1))
                        else:
                            wait_unit(phase, i, s)
                            wait_slot(phase, i, s)
                            if s < KT:
                                unit_mms([s % 4], [s % 4], HH, HL, tok)
                            elif s == KT:
                                unit_mms([s % 4], [s % 4], GH_, GL_, tok, lambda k: pe.wait_ge(
                                    g_done, KT + layer * CHUNKS * KT + i * KT + k + 1))
                            else:
                                unit_mms([s % 4], [s % 4], GH_, GL_, tok)

            mlp(0, "mlp0", TOK, 1)
            norm(2, TOK)

            def scores(i, gg, n):
                pp, j = n // 4, n % 4
                wide = WIDTH[j]
                loc = ROWS * wide
                if n >= 2:
                    pe.wait_ge(e_done, 16 * i + 8 * gg + n - 1)
                for hh in range(2):
                    bank = PSB[:, 2 * (n % 2) + hh, :]
                    rows = slice(64 * hh, 64 * hh + 64)
                    pe.matmul(bank[:, 0:loc], SELR[rows, :],
                              free(MSKR[rows, MASK_OF[j], 0:wide], [[1, wide], [0, ROWS]]),
                              start=True, stop=False, skip_group_check=True)
                    for p_, (qt, kt) in enumerate(((QH, KH), (QH, KL), (QL, KH))):
                        q = qt[rows, pp, P * j:P * (j + 1)]
                        at_ = 0
                        for a, b in KEYS[j]:
                            pe.matmul(bank[:, at_:at_ + b - a], q, kt[rows, pp, a:b], start=False, stop=False,
                                      skip_group_check=True)
                            at_ += b - a
                        mm = pe.matmul(bank[:, loc:loc + CTX], q, kt[rows, pp, LAT:TOK],
                                       start=False, stop=(p_ == 2), skip_group_check=True)
                mm.then_inc(s_mm, 1)

            def transposes(i, gg, n):
                j = n % 4
                wide = WIDTH[j]
                pe.wait_ge(p_done, 16 * i + 8 * gg + n + 1)
                if n >= 1:
                    pe.wait_ge(pt_done, 16 * i + 8 * gg + n + 1)
                for t in range(4):
                    for hh in range(2):
                        e = EE[:, n % 2, hh, :]
                        first = KEY_TILES[j][t][3] if t < 2 else ROWS * wide + (t - 2) * P
                        src = e[:, first:first + P]
                        mm = pe.transpose(PS[:, 2, (2 * t + hh) * P:(2 * t + hh + 1) * P], src, IDN)
                mm.then_inc(pt_mm, 1)

            def values(i, gg, n):
                pp, j = n // 4, n % 4
                pe.wait_ge(pt_done, 16 * i + 8 * gg + n + 2)
                if n >= 2:
                    pe.wait_ge(o_done, 16 * i + 8 * gg + n - 1 + 1)
                tiles = [kt[:3] for kt in KEY_TILES[j]] + [(4, 0, P), (5, 0, P)]
                for t, (vt, r0, r1) in enumerate(tiles):
                    for p_, (a, b) in enumerate(((VH, PTH), (VH, PTL), (VL, PTH))):
                        mm = pe.matmul(PSB[:, 6 + n % 2, 0:2 * P], a[r0:r1, vt, pp * P:(pp + 1) * P], b[r0:r1, t, :],
                                       start=(t == 0 and p_ == 0), stop=(t == 3 and p_ == 2), skip_group_check=True)
                mm.then_inc(o_mm, 1)

            pe.wait_ge(sel_set, 2)
            with pe.Fori(0, 2) as i:
                for gg in range(2):
                    for s in range(4):
                        wait_unit("attn", i, 6 * gg + s)
                        if s == 0:
                            pe.wait_ge(r_done, 16 * i + 8 * gg + 1)
                            pe.wait_ge(dve_evac, PRO + (3 + CHUNKS) * KT)
                        if s == 2:
                            pe.wait_ge(pt_done, 16 * i + 8 * gg + 1)
                        if s == 3:
                            pe.wait_ge(o_done, 16 * i + 8 * gg + 1)
                        unit_mms([s], [(6 * gg + s) % 4], HH, HL, LAT if s < 2 else TOK,
                                 (lambda k: pe.wait_ge(h_done, 2 * KT + k + 1)) if s == 0 else None)
                    wait_unit("attn", i, 6 * gg + 5)
                    a = (6 * gg + 4) % 4
                    for t in range(6):
                        if t == 0:
                            pe.wait_ge(qkv_done, 14 * i + 7 * gg + 1)
                        if t == 4:
                            pe.wait_ge(qkv_done, 14 * i + 7 * gg + 2)
                        for k in range(KT):
                            for p_, (ht, wt) in enumerate(((HH, WH), (HL, WH), (HH, WL))):
                                mm = pe.matmul(PSB[:, t // 2, (t % 2) * 256:(t % 2) * 256 + 256], ht[:, k, t * P:(t + 1) * P],
                                               wt[:, a:a + 2, k, :], start=(k == 0 and p_ == 0),
                                               stop=(k == KT - 1 and p_ == 2), skip_group_check=True)
                        if t % 2:
                            mm.then_inc(v_mm, 1)
                    pe.wait_ge(v_mm, 6 * i + 3 * gg + 3)
                    pe.nop().then_inc(units_done, 1)
                    pe.nop().then_inc(units_done, 1)
                    pe.wait_ge(qkv_done, 14 * i + 7 * gg + 7)
                    scores(i, gg, 0)
                    scores(i, gg, 1)
                    for n in range(8):
                        transposes(i, gg, n)
                        if n + 2 < 8:
                            scores(i, gg, n + 2)
                        values(i, gg, n)
            for s in range(KT):
                wait_unit("attn_out", 0, s)
                if s == 0:
                    pe.wait_ge(e_done, 32)
                if s < 4:
                    pe.wait_ge(o_done, 32 + 1)
                else:
                    wait_slot("attn_out", 0, s)
                unit_mms([s % 4], [s % 4], OH, OL, LAT)
            norm(3, LAT)
            mlp(1, "mlp1", LAT, 3)
            norm(4, LAT)
            for k in range(KT):
                pe.wait_ge(y_out, k + 1)
                if k >= 2:
                    pe.wait_ge(row_done, k - 1)
                for t in range(LAT // P):
                    mm = pe.transpose(PS[:, k % 2, t * P:(t + 1) * P], HF[:, k % 2, t * P:(t + 1) * P], IDN)
                mm.then_inc(yt_mm, 1)

        @block.scalar
        def _(act):
            act.dma_start(CO[:, :], consts).then_inc(const_in, 16)
            for t in range(1, TOK // P, 2):
                src = x[0, t * P:(t + 1) * P, :] if t < 4 else ctx[0, (t - 4) * P:(t - 3) * P, :]
                act.dma_start(XN[:, t, :], src).then_inc(x_in[t], 16)
            for k in range(1, KT, 2):
                act.dma_start(ADAF[:, k, :], ada_w[0, k * P:(k + 1) * P, 0:2 * D]).then_inc(af_in[k], 16)

            def split_hi(u, slot):
                act.wait_ge(w_in[slot % 2], 16 * u[1] + 16)
                act.wait_ge(units_done, u[0] + PRO - 3)
                act.activation(WH[:, slot, :, :], WR[:, slot % 2, :, :], ACT.Copy).then_inc(hi_done, 1)

            def split_ahead(phase, i, s):
                u = unit_index(phase, i, s + 2)
                half = {"conv_in": i * 6, "conv_out": U_CONV_OUT // 2, "mlp0": U_MLP[0] // 2 + i * 8,
                        "attn": U_ATTN // 2 + i * 6, "attn_out": U_ATTN_OUT // 2,
                        "mlp1": U_MLP[1] // 2 + i * 8}[phase] + (s + 2) // 2
                split_hi((u, half), (s + 2) % 4)

            def squares(n, k, wait, tok):
                act.wait_ge(*wait)
                if k >= 3:
                    act.wait_ge(ss_done, 7 * n + k - 2)
                dst = SS if k == 0 else SQ[:, k % 2, :]
                ins = act.activation(dst[:, 0:LAT], XL[:, k, :], ACT.Square)
                if tok > LAT:
                    ins = act.activation(dst[:, LAT:TOK], XC[:, k, :], ACT.Square)
                ins.then_inc(sq_done, 1)

            def norm(n, tok, ada):
                act.wait_ge(var_done, n + 1)
                act.activation(ST[:, 1, 0:tok // P], ST[:, 0, 0:tok // P], ACT.Sqrt).then_inc(sd_done, 1)
                if ada is not None:
                    act.wait_ge(am_set, 2 * (n + 1))
                for k in range(KT):
                    act.wait_ge(t1_done, n * KT + k + 1)
                    if ada is None:
                        if k >= 2:
                            act.wait_ge(yt_mm, k - 1)
                        act.activation(HF[:, k % 2, 0:LAT], T1[:, k % 2, 0:LAT], ACT.Copy,
                                       scale=PT_[:, 32 + k:33 + k]).then_inc(y_out, 1)
                        continue
                    layer, sh = ada
                    if k >= 2:
                        act.wait_ge(h_done, n * KT + k - 1)
                    act.activation(HF[:, k % 2, 0:LAT], T1[:, k % 2, 0:LAT], ACT.Identity,
                                   bias=ADA[:, layer, 0, sh + k:sh + k + 1],
                                   scale=AM[:, n, 0, k:k + 1]).then_inc(hf_lat, 1)
                    act.wait_ge(hf_lat, n * KT + k + 1)
                    if tok > LAT:
                        act.wait_ge(hf_ctx, n * KT + k + 1)
                    act.activation(HH[:, k, 0:tok], HF[:, k % 2, 0:tok], ACT.Copy).then_inc(h_hi, 1)

            act.wait_ge(par_t, 1)
            act.activation(PT_[:, 0:80], PS[:, 3, 0:80], ACT.Copy).then_inc(act_evac, 1)
            act.wait_ge(par_t, 2)
            act.activation(PT_[:, 80:176], PS[:, 3, 512:608], ACT.Copy).then_inc(act_evac, 1)
            act.wait_ge(act_evac, 2)
            act.activation(CT[:, 0, :], PT_[:, 64:80], ACT.Exp, scale=-1.0).then_inc(silu_e, 1)
            act.wait_ge(const_in, 16)
            act.activation(SELR[:, :], CO[:, P:2 * P], ACT.Copy).then_inc(sel_set, 1)
            act.activation(MSKR[:, :, :], CO[:, 2 * P:].rearrange("p (m c) -> p m c", m=3), ACT.Copy).then_inc(sel_set, 1)
            for k in range(KT):
                squares(0, k, (dve_evac, k + 1), TOK)
            split_hi((0, 0), 0)
            split_hi((1, 0), 1)
            norm(0, TOK, (0, 0))

            with act.Fori(0, 2) as i:
                for s in range(12):
                    split_ahead("conv_in", i, s)
                    t = s // 3
                    if s % 3 == 0:
                        act.wait_ge(units_done, PRO + 12 * i + s + 1)
                        act.activation(CS_[:, t % 2, :], PS[:, s % 4, 0:TOK], ACT.Copy).then_inc(act_evac, 1)
                    elif s % 3 == 1:
                        act.wait_ge(dve_evac, PRO + 8 * i + 2 * t + 1)
                        act.activation(YY[:, t % 2, 0:TOK + 1], UU[:, t % 2, 0:TOK + 1], ACT.Copy,
                                       scale=PT_[:, bass.ds(i * 4 + 40 + t, 1)]).then_inc(y_done, 1)
                    else:
                        act.wait_ge(dve_evac, PRO + 8 * i + 2 * t + 2)
                        act.activation(GH_[:, bass.ds(i * 4 + t, 1), :].rearrange("p a n -> p (a n)"),
                                       GF[:, t % 2, :], ACT.Copy).then_inc(g_hi, 1)
            for s in range(KT):
                split_ahead("conv_out", 0, s)
                squares(1, s, (dve_evac, PRO + 2 * KT + s + 1), TOK)
            norm(1, TOK, (0, 24))

            def mlp(layer, phase, tok, norm_next):
                tiles = KT + layer * CHUNKS * KT

                def chunk(i, last):
                    for s in range(2 * KT):
                        if not (last and layer == 1 and s >= 2 * KT - 2):
                            split_ahead(phase, i, s)
                        if s < KT:
                            act.wait_ge(units_done, unit_index(phase, i, s) + PRO + 1)
                            act.wait_ge(a_done, i * KT + layer * CHUNKS * KT + s + 1)
                            act.activation(RR[:, s % 2, 0:tok], PS[:, s % 4, 0:tok], ACT.Relu).then_inc(act_evac, 1)
                            act.wait_ge(act_evac, evac_counts(phase, i, s + 1)[0])
                            act.activation(GH_[:, s, 0:tok], RR[:, s % 2, 0:tok], ACT.Square).then_inc(g_hi, 1)
                        elif last:
                            squares(norm_next, s - KT, (dve_evac, evac_counts(phase, i, s + 1)[1]), tok)

                with act.Fori(0, CHUNKS - 1) as i:
                    chunk(i, False)
                chunk(CHUNKS - 1, True)

            mlp(0, "mlp0", TOK, 2)
            norm(2, TOK, (1, 0))

            with act.Fori(0, 2) as i:
                for gg in range(2):
                    def exps(n):
                        keys = ROWS * WIDTH[n % 4] + CTX
                        act.wait_ge(m_neg, 16 * i + 8 * gg + n + 2)
                        for hh in range(2):
                            ins = act.activation(EE[:, n % 2, hh, 0:keys], PSB[:, 2 * (n % 2) + hh, 0:keys], ACT.Exp,
                                                 bias=SM[:, n % 2, 2, hh:hh + 1], accum_out=SM[:, n % 2, 3, hh:hh + 1])
                        ins.then_inc(e_done, 1)

                    for s in range(4):
                        split_ahead("attn", i, 6 * gg + s)
                        act.wait_ge(units_done, PRO + U_ATTN + 12 * i + 6 * gg + s + 1)
                        if s < 2:
                            for a, b, to in Q_ORDER:
                                ins = act.activation(QH[:, s, to:to + b - a], PS[:, s, a:b], ACT.Copy, scale=ATTN_SCALE)
                            ins.then_inc(qk_hi, 1)
                        else:
                            act.activation(KH[:, s - 2, :], PS[:, s, 0:TOK], ACT.Copy).then_inc(qk_hi, 1)
                    for b in range(3):
                        act.wait_ge(v_mm, 6 * i + 3 * gg + b + 1)
                        act.activation(VH[:, 2 * b:2 * b + 2, :], PSB[:, b, :].rearrange("p (t n) -> p t n", t=2),
                                       ACT.Copy).then_inc(v_hi, 1)
                    exps(0)
                    exps(1)
                    split_ahead("attn", i, 6 * gg + 4)
                    split_ahead("attn", i, 6 * gg + 5)
                    for n in range(8):
                        pp, j = n // 4, n % 4
                        act.wait_ge(pt_mm, 16 * i + 8 * gg + n + 1)
                        act.activation(PTH[:, :, :].rearrange("p t n -> p (t n)"), PS[:, 2, :], ACT.Copy).then_inc(pt_hi, 1)
                        if n + 2 < 8:
                            exps(n + 2)
                        act.wait_ge(o_mm, 16 * i + 8 * gg + n + 1)
                        for hh in range(2):
                            rows = slice(64 * hh, 64 * hh + 64)
                            dst = OH[rows, bass.ds(i * 4 + 2 * gg + pp, 1), P * j:P * (j + 1)]
                            ins = act.activation(dst.rearrange("p a n -> p (a n)"),
                                                 PSB[rows, 6 + n % 2, hh * P:(hh + 1) * P], ACT.Copy)
                        ins.then_inc(o_hi, 1)
            for s in range(KT):
                split_ahead("attn_out", 0, s)
                squares(3, s, (dve_evac, PRO + (3 + CHUNKS) * KT + s + 1), LAT)
            norm(3, LAT, (1, 24))
            mlp(1, "mlp1", LAT, 4)
            norm(4, LAT, None)

        @block.vector
        def _(dve):
            def split_lo(u, slot):
                dve.wait_ge(hi_done, u + 1)
                dve.tensor_tensor(WL[:, slot, :, :], WR[:, slot % 2, :, :], WH[:, slot, :, :].bitcast(F32),
                                  ALU.subtract).then_inc(lo_done, 1)

            def split_ahead(phase, i, s):
                split_lo(unit_index(phase, i, s + 2), (s + 2) % 4)

            def sums(n, k, tok):
                if k == 0:
                    return
                dve.wait_ge(sq_done, n * KT + k + 1)
                if k >= 2:
                    dve.wait_ge(ss_done, 7 * n + k - 1)
                dve.tensor_tensor(SS[:, 0:tok], SS[:, 0:tok], SQ[:, k % 2, 0:tok], ALU.add).then_inc(ss_done, 1)

            def norm(n, tok, ada, meanwhile=None):
                nt = tok // P
                dve.wait_ge(ms_done, n + 1)
                dve.tensor_scalar(ST[:, 0, 0:nt], PS[:, 2, 0:nt], 1.0 / D, EPS, ALU.mult, ALU.add).then_inc(var_done, 1)
                dve.wait_ge(sd_done, n + 1)
                dve.reciprocal(ST[:, 2, 0:nt], ST[:, 1, 0:nt]).then_inc(rs_done, 1)
                dve.wait_ge(rs_done, n + 1)
                dve.tensor_tensor(DI[:, 0:nt, :], free(IDN, [[0, nt], [1, P]]),
                                  free(ST[:, 2, 0:nt], [[1, nt], [0, P]]), ALU.mult).then_inc(d_done, 1)
                if meanwhile:
                    meanwhile()
                dve.wait_ge(inv_done, n + 1)

                def t1(k):
                    if ada is None and k >= 2:
                        dve.wait_ge(y_out, k - 1)
                    if n == 2:
                        for a, dims in ((0, [[COLS - 8, 2], [1, 8], [COLS, ROWS]]), (8, [[1, COLS - 16], [COLS, ROWS]])):
                            ins = dve.tensor_tensor(T1[:, k % 2, a * WIN:a * WIN + ROWS * (16 if a == 0 else COLS - 16)],
                                                    free(XL[:, k, a:a + 1], dims), free(PS[:, 3, a:a + 1], dims), ALU.mult)
                    else:
                        ins = dve.tensor_tensor(T1[:, k % 2, 0:LAT], XL[:, k, :], PS[:, 3, 0:LAT], ALU.mult)
                    if tok > LAT:
                        ins = dve.tensor_tensor(T1[:, k % 2, LAT:TOK], XC[:, k, :], PS[:, 3, LAT:TOK], ALU.mult)
                    ins.then_inc(t1_done, 1)

                t1(0)
                for k in range(KT):
                    if ada is None:
                        if k + 1 < KT:
                            t1(k + 1)
                        dve.wait_ge(yt_mm, k + 1)
                        dve.tensor_copy(OUTB[:, k, :, :].rearrange("p t n -> p (t n)"), PS[:, k % 2, 0:LAT])\
                            .then_inc(row_done, 1)
                        continue
                    layer, sh = ada
                    if tok > LAT:
                        dve.wait_ge(t1_done, n * KT + k + 1)
                        if k >= 2:
                            dve.wait_ge(h_done, n * KT + k - 1)
                        dve.tensor_scalar(HF[:, k % 2, LAT:TOK], T1[:, k % 2, LAT:TOK], AM[:, n, 1, k:k + 1],
                                          ADA[:, layer, 1, sh + k:sh + k + 1], ALU.mult, ALU.add).then_inc(hf_ctx, 1)
                    if k + 1 < KT:
                        t1(k + 1)
                    dve.wait_ge(h_hi, n * KT + k + 1)
                    dve.tensor_tensor(HL[:, k, 0:tok], HF[:, k % 2, 0:tok], HH[:, k, 0:tok].bitcast(F32),
                                      ALU.subtract).then_inc(h_done, 1)

            def scale_terms(n, layer, gcol, sc, count):
                dve.wait_ge(ada_set, count)
                for cond in range(2):
                    dve.scalar_tensor_tensor(AM[:, n, cond, :], ADA[:, layer, cond, sc:sc + KT], 1.0,
                                             PT_[:, gcol:gcol + KT], ALU.add, ALU.mult).then_inc(am_set, 1)

            def ada_entry(layer, entry, half, slot, b, q, buf, blocks_reduced):
                dve.wait_ge(a_in[slot], 16 * half + 16)
                if q == 0:
                    dve.wait_ge(ada_red, blocks_reduced + 2)
                for kk in range(2):
                    for cond in range(2):
                        sc = CSI[:, 2 * q + kk, cond:cond + 1]
                        a = AC[:, buf, cond, :]
                        first = q == 0 and kk == 0
                        if kk:
                            dve.wait_ge(ada_step, entry * 3 + cond + 1)
                        elif not first:
                            dve.wait_ge(*((ada_used, entry + 2) if cond else (ada_step, entry * 3)))
                        if first:
                            ins = dve.tensor_scalar(a, AR[:, slot, kk, :], sc, None, ALU.mult)
                        else:
                            ins = dve.scalar_tensor_tensor(a, AR[:, slot, kk, :], sc, a, ALU.mult, ALU.add)
                        ins.then_inc(ada_used if kk and cond else ada_step, 1)

            def ada_out(layer, slot, tile):
                for cond in range(2):
                    dve.tensor_tensor(ADA[:, layer, cond, bass.ds(tile, 4)], PS[:, slot, TOK + 4 * cond:TOK + 4 * cond + 4],
                                      PT_[:, bass.ds(tile + 80 + 48 * layer, 4)], ALU.add).then_inc(ada_set, 1)

            def residual(slot, k, layer, gate, tok, by_column=False):
                y, xk = PS[:, slot, 0:LAT], XL[:, k, :]
                if by_column:
                    y = y.rearrange("p (c r) -> p r c", r=ROWS)
                    xk = xk.rearrange("p (r c) -> p r c", r=ROWS)
                ins = dve.scalar_tensor_tensor(xk, y, ADA[:, layer, 0, gate + k:gate + k + 1], xk, ALU.mult, ALU.add)
                if tok > LAT:
                    ins = dve.scalar_tensor_tensor(XC[:, k, :], PS[:, slot, LAT:TOK],
                                                   ADA[:, layer, 1, gate + k:gate + k + 1], XC[:, k, :], ALU.mult, ALU.add)
                ins.then_inc(dve_evac, 1)

            for what in (lo_done, lo_done, ada_used, ada_used, a_done, a_done, m_neg, r_done, pt_done, o_done):
                dve.engine_nop().then_inc(what, 1)
            dve.wait_ge(rpb_zero, 1)
            dve.wait_ge(rpb_in, 16)
            dve.tensor_copy(free(RPB[:, 711:712], [[-BPITCH, 15], [-1, 31]]), RPN[:, :, :]).then_inc(rpb_rev, 1)
            for k in range(KT):
                dve.wait_ge(units_done, k + 1)
                dve.tensor_copy(XL[:, k, :], PS[:, k % 4, 0:LAT])
                dve.tensor_copy(XC[:, k, :], PS[:, k % 4, LAT:TOK]).then_inc(dve_evac, 1)
                if k == 1:
                    dve.wait_ge(silu_e, 1)
                    dve.tensor_scalar(CT[:, 1, :], CT[:, 0, :], 1.0, None, ALU.add).then_inc(silu_d, 1)
                    dve.wait_ge(silu_d, 1)
                    dve.reciprocal(CT[:, 2, :], CT[:, 1, :]).then_inc(silu_r, 1)
                    dve.wait_ge(silu_r, 1)
                    dve.tensor_tensor(CSI[:, :, :], PT_[:, 64:80].rearrange("p (a k) -> p k a", a=2),
                                      CT[:, 2, :].rearrange("p (a k) -> p k a", a=2), ALU.mult).then_inc(silu_done, 1)
                if k >= 1:
                    sums(0, k - 1, TOK)
            sums(0, KT - 1, TOK)
            split_lo(0, 0)
            split_lo(1, 1)

            def first_ada():
                dve.wait_ge(ada_red, 2)
                for cond in range(2):
                    dve.tensor_tensor(ADA[:, 0, cond, 0:16], free(PS[:, 0, cond:cond + 1], [[2, 16]]), PT_[:, 80:96],
                                      ALU.add).then_inc(ada_set, 1)
                scale_terms(0, 0, 0, 8, 2)

            dve.wait_ge(scratch_in, 16)
            norm(0, TOK, (0, 0), first_ada)

            dve.wait_ge(h_done, KT)
            for col in (0, LAT + 1, TOK + 2):
                dve.memset(UU[:, :, col:col + 1], 0.0)
            with dve.Fori(0, 2) as i:
                n = 0
                for s in range(12):
                    split_ahead("conv_in", i, s)
                    for b, q in ADA_CONV[s]:
                        ada_entry(0, i * 16 + n, i * 8 + n // 2, n % 2, b, q, b % 2, i * 4 + b - 1)
                        n += 1
                    t = s // 3
                    if s % 3:
                        dve.wait_ge(units_done, PRO + 12 * i + s + 1)
                        if s in RED_CONV:
                            ada_out(0, s % 4, (i * 4 + 4 + RED_CONV[s]) * 4)
                    if s % 3 == 1:
                        if t:
                            dve.wait_ge(g_done, 4 * i + t)
                        dve.wait_ge(act_evac, evac_counts("conv_in", i, s)[0])
                        dve.tensor_tensor(UU[:, t % 2, 1:LAT + 1], PS[:, s % 4, 0:LAT], CS_[:, t % 2, 0:LAT], ALU.mult)
                        dve.tensor_tensor(UU[:, t % 2, LAT + 2:TOK + 2], PS[:, s % 4, LAT:TOK], CS_[:, t % 2, LAT:TOK],
                                          ALU.mult).then_inc(dve_evac, 1)
                    elif s % 3 == 2:
                        y = YY[:, t % 2, 0:TOK + 1]
                        dve.wait_ge(y_done, 4 * i + t + 1)
                        for tap in (1, 2):
                            dve.scalar_tensor_tensor(y, UU[:, t % 2, tap:tap + TOK + 1],
                                                     PT_[:, bass.ds(i * 4 + 40 + KT * tap + t, 1)], y,
                                                     ALU.mult, ALU.add).then_inc(y_mid, 1)
                            dve.wait_ge(y_mid, 8 * i + 2 * t + tap)
                        dve.tensor_tensor(GF[:, t % 2, 0:LAT], PS[:, s % 4, 0:LAT], YY[:, t % 2, 0:LAT], ALU.mult)
                        dve.tensor_tensor(GF[:, t % 2, LAT:TOK], PS[:, s % 4, LAT:TOK], YY[:, t % 2, LAT + 1:TOK + 1],
                                          ALU.mult).then_inc(dve_evac, 1)
                        dve.wait_ge(g_hi, 4 * i + t + 1)
                        hi = GH_[:, bass.ds(i * 4 + t, 1), :].bitcast(F32).rearrange("p a n -> p (a n)")
                        dve.tensor_tensor(GL_[:, bass.ds(i * 4 + t, 1), :].rearrange("p a n -> p (a n)"),
                                          GF[:, t % 2, :], hi, ALU.subtract).then_inc(g_done, 1)
            scale_terms(1, 0, 16, 32, 18)
            for s in range(KT):
                split_ahead("conv_out", 0, s)
                dve.wait_ge(units_done, PRO + U_CONV_OUT + s + 1)
                residual(s % 4, s, 0, 16, TOK)
                if s:
                    sums(1, s - 1, TOK)
            sums(1, KT - 1, TOK)
            norm(1, TOK, (0, 24))

            def mlp(layer, phase, tok, norm_next):
                tiles = layer * CHUNKS * KT

                def chunk(i, last):
                    n = 0
                    for s in range(2 * KT):
                        if not (last and layer == 1 and s >= 2 * KT - 2):
                            split_ahead(phase, i, s)
                        if layer == 0:
                            for b, q in ADA_MLP[s]:
                                ada_entry(1, i * 12 + 32 + n, i * 6 + 16 + n // 2, n % 2, b, q, b % 2,
                                          i * 3 + 8 + b - (b > 0))
                                n += 1
                        if s < KT:
                            dve.wait_ge(act_evac, evac_counts(phase, i, s + 1)[0])
                            dve.wait_ge(g_done, i * KT + KT + tiles + s - 1)
                            r = RR[:, s % 2, 0:tok]
                            dve.tensor_tensor(AA[:, s % 2, 0:tok], r, r, ALU.mult).then_inc(a_done, 1)
                            dve.wait_ge(a_done, i * KT + 2 + tiles + s + 1)
                            dve.wait_ge(g_hi, i * KT + KT + tiles + s + 1)
                            dve.tensor_tensor(GL_[:, s, 0:tok], AA[:, s % 2, 0:tok], GH_[:, s, 0:tok].bitcast(F32),
                                              ALU.subtract).then_inc(g_done, 1)
                        else:
                            dve.wait_ge(units_done, unit_index(phase, i, s) + PRO + 1)
                            if layer == 0 and s in RED_MLP:
                                ada_out(1, s % 4, (i * 3 + RED_MLP[s]) * 4)
                            residual(s % 4, s - KT, layer, 40, tok)
                            if last and s > KT:
                                sums(norm_next, s - KT - 1, tok)

                with dve.Fori(0, CHUNKS - 1) as i:
                    chunk(i, False)
                chunk(CHUNKS - 1, True)
                sums(norm_next, KT - 1, tok)

            mlp(0, "mlp0", TOK, 2)
            scale_terms(2, 1, KT, 8, 42)
            scale_terms(3, 1, 3 * KT, 32, 42)
            norm(2, TOK, (1, 0))

            with dve.Fori(0, 2) as i:
                for gg in range(2):
                    def maxima(n):
                        wide = WIDTH[n % 4]
                        loc = ROWS * wide
                        item = 16 * i + 8 * gg + n
                        b0 = 2 * (n % 2)
                        dve.wait_ge(s_mm, item + 1)
                        dve.reduce_max(SM[:, n % 2, 0, :], PSB[:, b0:b0 + 2, loc:loc + CTX], AX_X,
                                       negate=True).then_inc(m_ctx, 1)
                        for hh in range(2):
                            s_loc = PSB[:, b0 + hh, 0:loc].rearrange("p (c r) -> p c r", r=ROWS)
                            last = BRUN - 1 - (8 if n % 4 == 0 else 0)
                            bias = free(BT[:, 2 * (n // 4) + hh, last:last + 1], [[-1, wide], [-BPITCH, ROWS]])
                            dve.tensor_tensor_reduce(s_loc, s_loc, bias, 1.0, LOWEST, ALU.add,
                                                     ALU.max, SM[:, n % 2, 1, hh:hh + 1]).then_inc(m_all, 1)
                        dve.wait_ge(m_all, 32 * i + 16 * gg + 2 * n + 2)
                        dve.wait_ge(m_ctx, item + 1)
                        dve.scalar_tensor_tensor(SM[:, n % 2, 2, :], SM[:, n % 2, 1, :], -1.0, SM[:, n % 2, 0, :],
                                                 ALU.mult, ALU.min).then_inc(m_neg, 1)

                    def recip(n):
                        dve.wait_ge(e_done, 16 * i + 8 * gg + n + 1)
                        dve.reciprocal(SM[:, n % 2, 4, :], SM[:, n % 2, 3, :]).then_inc(r_done, 1)

                    for s in range(4):
                        split_ahead("attn", i, 6 * gg + s)
                        dve.wait_ge(qk_hi, 8 * i + 4 * gg + s + 1)
                        if s < 2:
                            for a, b, to in Q_ORDER:
                                ins = dve.scalar_tensor_tensor(
                                    QL[:, s, to:to + b - a], PS[:, s, a:b], ATTN_SCALE,
                                    QH[:, s, to:to + b - a].bitcast(F32), ALU.mult, ALU.subtract)
                            ins.then_inc(qkv_done, 1)
                        else:
                            dve.tensor_tensor(KL[:, s - 2, :], PS[:, s, 0:TOK], KH[:, s - 2, :].bitcast(F32),
                                              ALU.subtract).then_inc(qkv_done, 1)
                    for b in range(3):
                        dve.wait_ge(v_hi, 6 * i + 3 * gg + b + 1)
                        dve.tensor_tensor(VL[:, 2 * b:2 * b + 2, :], PSB[:, b, :].rearrange("p (t n) -> p t n", t=2),
                                          VH[:, 2 * b:2 * b + 2, :].bitcast(F32), ALU.subtract).then_inc(qkv_done, 1)
                    dve.wait_ge(bias_in, 32 * i + 16 * gg + 16)
                    maxima(0)
                    recip(0)
                    maxima(1)
                    split_ahead("attn", i, 6 * gg + 4)
                    split_ahead("attn", i, 6 * gg + 5)
                    for n in range(8):
                        pp, j = n // 4, n % 4
                        dve.wait_ge(pt_hi, 16 * i + 8 * gg + n + 1)
                        dve.tensor_tensor(PTL[:, :, :].rearrange("p t n -> p (t n)"), PS[:, 2, :],
                                          PTH[:, :, :].bitcast(F32).rearrange("p t n -> p (t n)"),
                                          ALU.subtract).then_inc(pt_done, 1)
                        if n + 1 < 8:
                            recip(n + 1)
                        if n + 2 < 8:
                            maxima(n + 2)
                        dve.wait_ge(o_hi, 16 * i + 8 * gg + n + 1)
                        for hh in range(2):
                            rows = slice(64 * hh, 64 * hh + 64)
                            ft = bass.ds(i * 4 + 2 * gg + pp, 1)
                            lo, hi = (o.rearrange("p a n -> p (a n)") for o in
                                      (OL[rows, ft, P * j:P * (j + 1)], OH[rows, ft, P * j:P * (j + 1)].bitcast(F32)))
                            ins = dve.tensor_tensor(lo, PSB[rows, 6 + n % 2, hh * P:(hh + 1) * P], hi, ALU.subtract)
                        ins.then_inc(o_done, 1)
            for s in range(KT):
                split_ahead("attn_out", 0, s)
                dve.wait_ge(units_done, PRO + U_ATTN_OUT + s + 1)
                residual(s % 4, s, 1, 16, LAT, by_column=True)
                if s:
                    sums(3, s - 1, LAT)
            sums(3, KT - 1, LAT)
            norm(3, LAT, (1, 24))
            mlp(1, "mlp1", LAT, 4)
            norm(4, LAT, None)


_INS = ["x", "c", "ctx", "c_ctx", "norm1_g", "norm2_g", "ada_w", "ada_b", "conv_in_w", "conv_w", "conv_out_w",
        "attn_qkv_w", "attn_rpb", "attn_out_w", "mlp_w1", "mlp_w2", "final_g"]
_OUTS = [((1, 512, 1024), "float32")]


def kernel(**inputs):
    import numpy as _np
    import concourse.bacc as _bacc
    from concourse import mybir as _mybir
    from concourse.bass_utils import run_bass_kernel_spmd as _run

    nc = _bacc.Bacc("TRN2", target_bir_lowering=False, num_devices=1)
    arrays, args = {}, []
    for name in _INS:
        a = _np.ascontiguousarray(inputs[name])
        arrays[f"in_{name}_dram"] = a
        args.append(nc.dram_tensor(f"in_{name}_dram", a.shape, _mybir.dt.from_np(a.dtype), kind="ExternalInput").ap())
    arrays["consts_dram"] = constants()
    args.append(nc.dram_tensor("consts_dram", (P, NCONST), _mybir.dt.float32, kind="ExternalInput").ap())
    for i, (shape, dtype) in enumerate(_OUTS):
        dt = _mybir.dt.from_np(_np.dtype(dtype))
        args.append(nc.dram_tensor(f"out_{i}_dram", shape, dt, kind="ExternalOutput").ap())
    build(nc, *args)
    r = _run(nc, [arrays], core_ids=[0])
    return r.results[0]["out_0_dram"]
```

```python
from contextlib import ExitStack

import numpy as np

import concourse.bass as bass
from concourse import mybir

F32 = mybir.dt.float32
F32R = mybir.dt.float32r
ALU = mybir.AluOpType
ACT = mybir.ActivationFunctionType
AX_X = mybir.AxisListType.X

P = 128
D = 1024
KT = D // P
LAT, CTX = 512, 256
TOK = LAT + CTX
ROWS, COLS = 8, 64
HEADS, DH = 16, 64
WIN = 16
F = 4 * D
CHUNKS = F // D
EPS = 1e-6
MASKED = -1e30
LOWEST = -3.0e38
ATTN_SCALE = DH ** -0.5

U_CONV_IN = 0
U_CONV_OUT = U_CONV_IN + 3 * KT
U_MLP = [U_CONV_OUT + KT, 0]
U_ATTN = U_MLP[0] + 2 * KT * CHUNKS
U_ATTN_OUT = U_ATTN + 3 * KT
U_MLP[1] = U_ATTN_OUT + KT
UNITS = U_MLP[1] + 2 * KT * CHUNKS
PRO = KT

WIDTH = [24, 32, 32, 24]
KEYS = [[(0, 64), (128, 256)], [(128, 384)], [(256, 512)], [(384, 512), (64, 128)]]
KEY_TILES = [
    [(0, 0, 64, 0), (1, 0, 128, 64)],
    [(1, 0, 128, 0), (2, 0, 128, 128)],
    [(2, 0, 128, 0), (3, 0, 128, 128)],
    [(3, 0, 128, 0), (0, 64, 128, 64)],
]
Q_ORDER = [(0, 64, 0), (128, 512, 64), (64, 128, 448)]
MASK_OF = [0, 1, 1, 2]
GROUPS = 4
PARTS = {0: [("q", 1)], 1: [("k_lat", 1), ("k_ctx", 1)], 2: [("q", 2)], 3: [("k_lat", 2)], 4: [("k_ctx", 2)],
         5: [("v", 0)], 6: [("v", 1)], 7: [("v", 2)]}
PARTS_FIRST, PARTS_GROUP = 6, 9
PARTS_ALL = PARTS_FIRST + PARTS_GROUP * (GROUPS - 1) + 3
UNIT_PARTS = [1, 3, 4, 6, 9, 9]
BPITCH = 47
BHEAD = 15 * BPITCH + 15
BRUN = ROWS * BPITCH


def constants():
    ident = np.eye(P, dtype=np.float32)
    sel = np.zeros((P, P), np.float32)
    mask = np.zeros((P, 3, 32), np.float32)
    for half in (0, 64):
        for qc in range(WIN):
            sel[half + qc, qc * ROWS:(qc + 1) * ROWS] = 1.0
            for m, start in enumerate((max(qc - 8, 0), qc, min(qc, 8))):
                mask[half + qc, m, :] = MASKED
                mask[half + qc, m, start:start + WIN] = 0.0
    return np.ascontiguousarray(np.concatenate(
        [ident, sel, mask.reshape(P, 96), np.tile(np.eye(32, dtype=np.float32), (4, 4))], axis=1))


NCONST = 2 * P + 96


def free(view, dims):
    return bass.AP(view.tensor, view.offset, [list(view.ap[0])] + dims)


def build(nc, x, c, ctx, c_ctx, norm1_g, norm2_g, ada_w, ada_b, conv_in_w, conv_w, conv_out_w,
          attn_qkv_w, attn_rpb, attn_out_w, mlp_w1, mlp_w2, final_g, consts, out):
    base = (nc.sbuf_base + 63) // 64 * 64

    def at(name, shape, dt, word):
        assert base + 4 * (word + int(np.prod(shape[1:]))) <= nc.sbuf_usable_end, name
        return nc.alloc_sbuf_tensor_at(name, shape, dt, offset=base + 4 * word)

    o_x = 0
    o_h = o_x + KT * TOK
    o_g = o_h + 2 * KT * TOK
    o_s = o_g + 2 * KT * TOK
    o_wr = o_s + 6400
    o_ar = o_wr + 2 * KT * P
    o_wh = o_ar + 2 * KT * P
    o_wl = o_wh + 4 * KT * P
    o_acc = o_wl + 4 * KT * P
    o_misc = o_acc + 2 * 2 * 512

    XL = at("x_latent", [P, KT, LAT], F32, o_x)
    XC = at("x_context", [P, KT, CTX], F32, o_x + KT * LAT)
    BT = at("bias_rows", [P, 2, 2, BRUN], F32, o_x + KT * LAT)
    HH = at("h_hi", [P, KT, TOK], F32R, o_h)
    HL = at("h_lo", [P, KT, TOK], F32R, o_h + KT * TOK)
    XN = at("x_rows", [P, TOK // P, D], F32, o_h)
    PRA = at("param_rows_a", [80, P], F32, o_h + KT * TOK)
    PRB = at("param_rows_b", [96, P], F32, o_h + KT * TOK + P)
    RPB = at("rpb_reversed", [HEADS, BHEAD], F32, o_h + KT * TOK + 2 * P)
    RPN = at("rpb_rows", [HEADS, 15, 31], F32, o_h + KT * TOK + 2 * P + BHEAD)
    OUTB = at("out_rows", [P, KT, LAT // P, P], F32, o_h)
    GH_ = at("g_hi", [P, KT, TOK], F32R, o_g)
    GL_ = at("g_lo", [P, KT, TOK], F32R, o_g + KT * TOK)
    ADAF = at("ada_first", [P, KT, 2 * D], F32, o_g)
    OH = at("o_hi", [P, KT, LAT], F32R, o_g)
    OL = at("o_lo", [P, KT, LAT], F32R, o_g + KT * LAT)
    QH = at("q_hi", [P, 2, LAT], F32R, o_g + 2 * KT * LAT)
    QL = at("q_lo", [P, 2, LAT], F32R, o_g + 2 * KT * LAT + 2 * LAT)
    PTH = at("pt_hi", [P, 4, 2 * P], F32R, o_g + 2 * KT * LAT + 4 * LAT)
    PTL = at("pt_lo", [P, 4, 2 * P], F32R, o_g + 2 * KT * LAT + 4 * LAT + 8 * P)
    KH = at("k_hi", [P, 2, TOK], F32R, o_s)
    KL = at("k_lo", [P, 2, TOK], F32R, o_s + 2 * TOK)
    o_end = o_misc + NCONST + 2 * P + 96 + 496
    v_at = [[[o_s + 4 * TOK + 12 * P * part + 4 * P * b for b in range(3)] for part in range(2)],
            [[o_ar, o_ar + 4 * P, o_ar + 8 * P], [o_ar + 12 * P, o_x + KT * LAT + 4 * BRUN, o_end]]]
    VH, VL = ([[at(f"v_{what}{buf}_{b}", [P, 2, 2 * P], F32R, v_at[buf][part][b]) for b in range(3)]
               for buf in range(2)] for part, what in enumerate(("hi", "lo")))
    CS_ = at("conv_c", [P, 2, TOK], F32, o_s)
    UU = at("conv_u", [P, 2, TOK + 8], F32, o_s + 2 * TOK)
    YY = at("conv_y", [P, 2, TOK + 8], F32, o_s + 4 * TOK + 16)
    GF = at("conv_g", [P, 2, TOK], F32, o_s + 6 * TOK + 32)
    RR = at("relu", [P, 2, TOK], F32, o_s)
    AA = at("relu2", [P, 2, TOK], F32, o_s + 2 * TOK)
    T1 = at("normed", [P, 2, TOK], F32, o_s)
    HF = at("modulated", [P, 2, TOK], F32, o_s + 2 * TOK)
    AROW = at("ada_first_rows", [2, 4, 512], F32, o_s + 2 * TOK)
    SQ = at("squares", [P, 2, TOK], F32, o_s + 4096)
    SS = at("square_sums", [P, TOK], F32, o_s + 4096 + 2 * TOK)
    WR = at("w_raw", [P, 2, KT, P], F32, o_wr)
    AR = at("ada_raw", [P, 2, 2, 512], F32, o_ar)
    WH = at("w_hi", [P, 4, KT, P], F32R, o_wh)
    WL = at("w_lo", [P, 4, KT, P], F32R, o_wl)
    AC = at("ada_acc", [P, 2, 512], F32, o_acc)
    AT = at("ada_turned", [P, 2, 512], F32, o_acc + 1024)
    DI = at("inv_diag", [P, TOK // P, P], F32, o_acc)
    EE = at("probs", [P, 2, 2, 512], F32, o_acc)
    w = o_misc
    CO = at("consts", [P, NCONST], F32, w)
    w += NCONST
    SELR = at("selector", [P, P], F32R, w)
    w += P
    MSKR = at("window_masks", [P, 3, 32], F32R, w)
    w += 96
    ONES = at("ones", [P, P], F32, w)
    w += P
    PT_ = at("params", [P, 176], F32, w)
    w += 176
    ADA = at("ada", [P, 2, 2, 48], F32, w)
    w += 192
    AM = at("scale_terms", [P, 4, 2, KT], F32, w)
    w += 64
    CSI = at("silu_c", [P, KT, 2], F32, w)
    w += 16
    FOLD = at("fold", [P, P], F32, o_end)
    AQ = at("ada_quarters", [P, 4, 32], F32, o_end + P)
    CT = at("silu_tmp", [P, 3, 16], F32, o_acc + 1024)
    RMS = at("rms", [P, 2, 8], F32, w)
    w += 16
    EPSC = at("epsilon", [P, 1], F32, w)
    w += 8
    SM = at("softmax_small", [P, 2, 5, 2], F32, w)
    assert w <= o_end
    IDN = CO[:, 0:P]

    scratch = nc.dram_tensor("rpb_scratch", (HEADS, BHEAD), F32).ap()

    bias_rows = nc.dram_tensor("bias_rows_dram", (P, HEADS, BRUN), F32).ap()

    with ExitStack() as es:
        PS = es.enter_context(nc.psum_tensor("ps", [P, 4, 1024], F32))
        PSB = PS[:, :, :].rearrange("p s (b n) -> p (s b) n", b=2)

        def sem(name):
            return es.enter_context(nc.semaphore(name))

        x_in = [sem(f"x_in{t}") for t in range(TOK // P)]
        pa_in, pb_in, const_in, fold_in, rpb_in, scratch_in = map(sem, (
            "pa_in", "pb_in", "const_in", "fold_in", "rpb_in", "scratch_in"))
        af_in = [sem(f"ada_first_in{k}") for k in range(KT)]
        w_in = [sem(f"w_in{s}") for s in range(2)]
        a_in = [sem(f"ada_in{s}") for s in range(2)]
        rows_in, out_done = map(sem, ("rows_in", "out_done"))
        bias_in = [sem(f"bias_in{b}") for b in range(2)]
        ones_set, rpb_zero, rpb_rev, par_t, sel_set, silu_e, silu_d, silu_r, silu_done, af_mm, af_rows = map(sem, (
            "ones_set", "rpb_zero", "rpb_rev", "par_t", "sel_set", "silu_e", "silu_d", "silu_r", "silu_done",
            "ada_first_mm", "ada_first_rows"))
        hi_done, lo_done, units_done, act_evac, dve_evac = map(sem, (
            "hi_done", "lo_done", "units_done", "act_evac", "dve_evac"))
        ada_used, ada_red, ada_step, ada_turned, ada_part, ada_set, am_set = map(sem, (
            "ada_used", "ada_red", "ada_step", "ada_turned", "ada_part", "ada_set", "am_set"))
        sq_done, ss_done, ms_done, rms_done, rec_done, diag_done, inv_done = map(sem, (
            "sq_done", "ss_done", "ms_done", "rms_done", "rec_done", "diag_done", "inv_done"))
        t1_done, hf_lat, hf_ctx, h_hi, h_done = map(sem, ("t1_done", "hf_lat", "hf_ctx", "h_hi", "h_done"))
        y_done, y_mid, g_hi, g_done, a_done = map(sem, ("y_done", "y_mid", "g_hi", "g_done", "a_done"))
        part_mm, part_hi, part_done = map(sem, ("part_mm", "part_hi", "part_done"))
        s_mm, m_ctx, m_all, m_neg, e_done, r_done, p_done, pt_mm, pt_hi, pt_done, o_mm, o_hi, o_done = map(sem, (
            "s_mm", "m_ctx", "m_all", "m_neg", "e_done", "r_done", "p_done", "pt_mm", "pt_hi", "pt_done",
            "o_mm", "o_hi", "o_done"))
        y_out, yt_mm, row_done = map(sem, ("y_out", "yt_mm", "row_done"))

        block = es.enter_context(nc.Block())

        def norm_count(n):
            return 2 * min(n, 3) + max(n - 3, 0)

        SEG = {TOK: [(0, LAT), (LAT, TOK)], LAT: [(0, LAT)]}

        def evac_counts(phase, i, s):
            if phase == "conv_in":
                return 2 + i * 4 + (s + 2) // 3, PRO + i * 8 + (s - (s + 2) // 3)
            if phase == "conv_out":
                n = min(s, 0)
                return 2 + KT + (n + 2) // 3, PRO + 2 * KT + s - (n + 2) // 3
            a, d = {"mlp0": (2 + KT, PRO + 3 * KT), "mlp1": (2 + KT + CHUNKS * KT, PRO + (4 + CHUNKS) * KT),
                    "attn_out": (2 + KT + CHUNKS * KT, PRO + (3 + CHUNKS) * KT)}[phase]
            if phase == "attn_out":
                return a, d + s
            return a + i * KT + min(max(s, 0), KT), d + i * KT + min(s, 0) + max(s - KT, 0)

        def part_count(g, n):
            return PARTS_FIRST + PARTS_GROUP * g + sum(len(PARTS[m]) for m in range(n))

        def parts(g, n):
            return [part for part in PARTS[n] if g < GROUPS - 1 or part[1] == 1 and part[0] != "v"]

        def parts_of_unit(u):
            return (1, 3, 6, 6)[u] if u < 4 else PARTS_FIRST + PARTS_GROUP * ((u - 4) // 6) + UNIT_PARTS[(u - 4) % 6]

        def item_pair(g, n):
            return 2 * g + n // 4

        def unit_index(phase, i, s):
            return {"conv_in": U_CONV_IN + i * 12, "conv_out": U_CONV_OUT, "mlp0": U_MLP[0] + i * 16,
                    "attn": U_ATTN + i * 12, "attn_out": U_ATTN_OUT, "mlp1": U_MLP[1] + i * 16}[phase] + s

        ADA_CONV = [[(0, 0), (0, 1)], [(0, 2)], [(0, 3)], [(1, 0)], [(1, 1)], [(1, 2), (1, 3)],
                    [(2, 0)], [(2, 1)], [(2, 2)], [(2, 3)], [], []]
        RED_CONV = {4: 0, 8: 1, 11: 2}
        ADA_OUT = [[(0, 0), (0, 1)], [(0, 2)], [(0, 3), (1, 0)], [(1, 1), (1, 2)], [(1, 3)], [], [], []]
        RED_OUT = {4: 0, 7: 1}
        ADA_MLP = [[(s // 4, s % 4)] if s < 12 else [] for s in range(16)]
        RED_MLP = {8: 0, 10: 1, 14: 2}

        @block.sync
        def _(sp):
            for r, src in ((0, norm1_g.rearrange("l (k p) -> (l k) p", p=P)),
                           (16, norm2_g.rearrange("l (k p) -> (l k) p", p=P)),
                           (32, final_g.rearrange("(k p) -> k p", p=P))):
                sp.dma_start(PRA[r:r + src.shape[0], :], src).then_inc(pa_in, 16)
            sp.dma_start(PRB[:, :], ada_b.rearrange("l (k p) -> (l k) p", p=P)).then_inc(pb_in, 16)
            for t in range(0, TOK // P, 2):
                src = x[0, t * P:(t + 1) * P, :] if t < 4 else ctx[0, (t - 4) * P:(t - 3) * P, :]
                sp.dma_start(XN[:, t, :], src).then_inc(x_in[t], 16)
            for k in range(0, KT, 2):
                sp.dma_start(ADAF[:, k, :], ada_w[0, k * P:(k + 1) * P, 0:2 * D]).then_inc(af_in[k], 16)

            def load(phase, i, s, src):
                u = unit_index(phase, i, s)
                sp.wait_ge(lo_done, u + 1)
                sp.dma_start(WR[:, s % 2, :, :], src).then_inc(w_in[s % 2], 16)

            cin = conv_in_w[0].rearrange("(k p) n -> p k n", p=P)
            with sp.Fori(1, 3) as i1:
                i = i1 - 1
                for s in range(12):
                    col = (D, 2 * D, 0)[s % 3]
                    load("conv_in", i, s, cin[:, :, bass.ds(i1 * (4 * P) + (s // 3 - 4) * P + col, P)])
            cout = conv_out_w[0].rearrange("(k p) n -> p k n", p=P)
            for s in range(KT):
                load("conv_out", 0, s, cout[:, :, s * P:(s + 1) * P])

            def mlp(layer, phase):
                w1 = mlp_w1[layer].rearrange("(k p) n -> p k n", p=P)
                w2 = mlp_w2[layer].rearrange("(k p) n -> p k n", p=P)
                with sp.Fori(0, CHUNKS) as i:
                    for s in range(KT):
                        load(phase, i, s, w1[:, :, bass.ds(i * D + s * P, P)])
                    for s in range(KT):
                        load(phase, i, KT + s, w2[:, bass.ds(i * KT, KT), s * P:(s + 1) * P])

            mlp(0, "mlp0")
            qkv = attn_qkv_w[0].rearrange("(k p) n -> p k n", p=P)
            def bias_rows_load(pair):
                if pair >= 2:
                    sp.wait_ge(m_neg, 4 * (pair - 1))
                sp.dma_start(BT[:, pair % 2, :, :], bias_rows[:, 2 * pair:2 * pair + 2, :]).then_inc(bias_in[pair % 2], 16)

            def load_qkv(u, what, tile):
                load("attn", 0, u, qkv[:, :, what * D + tile * P:what * D + (tile + 1) * P])

            load_qkv(0, 0, 0)
            load_qkv(1, 1, 0)
            load_qkv(2, 2, 0)
            load_qkv(3, 2, 1)
            sp.wait_ge(rows_in, 16 * ROWS)
            sp.wait_ge(h_done, 3 * KT)
            bias_rows_load(0)
            bias_rows_load(1)
            for g in range(GROUPS):
                u = 4 + 6 * g
                load_qkv(u, 0, 2 * g + 1)
                load_qkv(u + 1, 1, 2 * g + 1)
                if g < GROUPS - 1:
                    load_qkv(u + 2, 0, 2 * g + 2)
                if g:
                    bias_rows_load(2 * g + 1)
                if g < GROUPS - 1:
                    load_qkv(u + 3, 1, 2 * g + 2)
                    load_qkv(u + 4, 2, 2 * g + 2)
                    bias_rows_load(2 * g + 2)
                    load_qkv(u + 5, 2, 2 * g + 3)
            aout = attn_out_w[0].rearrange("(k p) n -> p k n", p=P)
            for s in range(KT):
                load("attn_out", 0, s, aout[:, :, s * P:(s + 1) * P])
            mlp(1, "mlp1")
            for k in range(KT):
                sp.wait_ge(row_done, k + 1)
                sp.dma_start(out[0].rearrange("(t p) n -> p t n", p=P)[:, :, k * P:(k + 1) * P],
                             OUTB[:, k, :, :]).then_inc(out_done, 16)
            sp.wait_ge(out_done, 16 * KT)

        @block.gpsimd
        def _(pool):
            pool.memset(ONES[:, :], 1.0).then_inc(ones_set, 1)
            pool.memset(EPSC[:, :], EPS).then_inc(ones_set, 1)
            pool.memset(RPB[:, :], 0.0).then_inc(rpb_zero, 1)
            pool.dma_start(RPN[:, :, :], attn_rpb[0]).then_inc(rpb_in, 16)
            pool.wait_ge(rpb_rev, 1)
            pool.dma_start(scratch, RPB[:, :]).then_inc(scratch_in, 16)
            pool.wait_ge(scratch_in, 16)
            for qr in range(ROWS):
                src = bass.AP(scratch.tensor, qr * BPITCH, [[1, WIN], [BHEAD, HEADS], [1, BRUN]])
                pool.dma_start(bias_rows.rearrange("(c r) h n -> r c h n", r=ROWS)[qr], src).then_inc(rows_in, 16)

            def ada_load(layer, entry, slot, block_, quarter):
                pool.wait_ge(ada_used, entry + 1)
                src = ada_w[layer].rearrange("(q k p) n -> p q k n", p=P, k=2)[:, quarter, :, bass.ds(block_ * 512, 512)]
                pool.dma_start(AR[:, slot, :, :], src).then_inc(a_in[slot], 16)

            with pool.Fori(0, 2) as i:
                n = 0
                for entries in ADA_CONV:
                    for b, q in entries:
                        ada_load(0, i * 12 + n, n % 2, i * 3 + 4 + b, q)
                        n += 1
            for n, (b, q) in enumerate(sum(ADA_OUT, [])):
                ada_load(0, 24 + n, n % 2, 10 + b, q)
            with pool.Fori(0, 4) as i:
                n = 0
                for entries in ADA_MLP:
                    for b, q in entries:
                        ada_load(1, i * 12 + 32 + n, n % 2, i * 3 + b, q)
                        n += 1
            with pool.Fori(0, 4) as i:
                for n in range(8):
                    j = n % 4
                    keys = ROWS * WIDTH[j] + CTX
                    pool.wait_ge(r_done, i * 8 + n + 1)
                    e = EE[:, n % 2, :, 0:keys]
                    pool.tensor_tensor(e, e, free(SM[:, n % 2, 4, 0:1], [[1, 2], [0, keys]]), ALU.mult)\
                        .then_inc(p_done, 1)

        @block.tensor
        def _(pe):
            def unit_mms(slot, wslots, hi, lo, tok, ready=None):
                segs = SEG[tok]
                for k in range(KT):
                    for p_ in range(3):
                        wt, rt = ((WH, hi), (WL, hi), (WH, lo))[p_]
                        if ready and p_ != 1:
                            pe.wait_ge(ready[p_ // 2], ready[2] + k + 1)
                        for sl, ws in zip(slot, wslots):
                            for a, b in segs:
                                mm = pe.matmul(PS[:, sl, a:b], wt[:, ws, k, :], rt[:, k, a:b],
                                               start=(k == 0 and p_ == 0), stop=(k == KT - 1 and p_ == 2))
                            if k == KT - 1 and p_ == 2:
                                mm.then_inc(units_done, 1)

            def wait_unit(phase, i, s):
                u = unit_index(phase, i, s)
                pe.wait_ge(lo_done, u + 3)

            def wait_slot(phase, i, s):
                a, d = evac_counts(phase, i, s - 3)
                pe.wait_ge(act_evac, a)
                pe.wait_ge(dve_evac, d)

            def reduce_ada(block_, buf, slot):
                pe.wait_ge(ada_part, block_ + 1)
                pe.matmul(PS[:, slot, TOK:TOK + 32], FOLD[:, :], AQ[:, buf, :], start=True, stop=True).then_inc(ada_red, 1)

            def norm(n, tok):
                pe.wait_ge(ss_done, 6 * (n + 1))
                for sq in (SS, SQ[:, 1, :]):
                    if sq is not SS:
                        pe.wait_ge(sq_done, KT * (n + 1))
                    for g, (a, b) in enumerate(SEG[tok]):
                        for t in range(a // P, b // P):
                            mm = pe.matmul(PS[:, 2, g * 512 + t:g * 512 + t + 1], sq[:, t * P:(t + 1) * P], ONES[:, 0:1],
                                           start=(sq is SS and t == a // P), stop=(sq is not SS), skip_group_check=True)
                        if sq is not SS:
                            mm.then_inc(ms_done, 1)

            def norm_inverse(n, tok):
                for g, (a, b) in enumerate(SEG[tok]):
                    pe.wait_ge(diag_done, norm_count(n) + g + 1)
                    pe.matmul(PS[:, 3, a:b], ONES[:, :], DI[:, a // P:b // P, :], start=True, stop=True)\
                        .then_inc(inv_done, 1)

            pe.wait_ge(const_in, 16)
            pe.wait_ge(pa_in, 96)
            pe.transpose(PS[:, 3, 0:80], PRA[:, :], CO[0:80, 0:80]).then_inc(par_t, 1)
            pe.wait_ge(pb_in, 16)
            pe.transpose(PS[:, 3, 512:512 + 96], PRB[:, :], CO[0:96, 0:96]).then_inc(par_t, 1)
            for k in range(KT):
                if k == 3:
                    pe.wait_ge(act_evac, 2)
                if k >= 4:
                    pe.wait_ge(dve_evac, k - 3)
                for t in range(TOK // P):
                    if k == 0:
                        pe.wait_ge(x_in[t], 16)
                    mm = pe.transpose(PS[:, k % 4, t * P:(t + 1) * P], XN[:, t, k * P:(k + 1) * P], IDN)
                mm.then_inc(units_done, 1)
            pe.wait_ge(ones_set, 2)
            pe.wait_ge(silu_done, 1)
            pe.wait_ge(dve_evac, 6)
            for k in range(KT):
                pe.wait_ge(af_in[k], 16)
                for n in range(4):
                    mm = pe.matmul(PSB[0:2, n, :], CSI[:, k, :], ADAF[:, k, n * 512:(n + 1) * 512],
                                   start=(k == 0), stop=(k == KT - 1), skip_group_check=True)
                    if k == KT - 1:
                        mm.then_inc(af_mm, 1)
                if k == 3:
                    norm(0, TOK)
                if k == 5:
                    norm_inverse(0, TOK)
            for n in range(16):
                if n % 8 == 0:
                    pe.wait_ge(af_rows, n // 8 + 1)
                mm = pe.transpose(PS[:, 2, 2 * n:2 * n + 2], AROW[:, n // 4, n % 4 * P:(n % 4 + 1) * P], CO[0:2, 0:2])
                if n % 8 == 7:
                    mm.then_inc(ada_red, 3)

            pe.wait_ge(fold_in, 16)
            with pe.Fori(0, 2) as i:
                for s in range(12):
                    if s == 1:
                        continue
                    if s in RED_CONV:
                        wait_slot("conv_in", i, s)
                        reduce_ada(i * 3 + RED_CONV[s], RED_CONV[s], s % 4)
                    if s == 0:
                        wait_unit("conv_in", i, 1)
                        wait_slot("conv_in", i, 1)
                        unit_mms([0, 1], [0, 1], HH, HL, TOK, (h_hi, h_done, 0))
                    else:
                        wait_unit("conv_in", i, s)
                        wait_slot("conv_in", i, s)
                        unit_mms([s % 4], [s % 4], HH, HL, TOK)
            for s in range(KT):
                wait_unit("conv_out", 0, s)
                wait_slot("conv_out", 0, s)
                if s in RED_OUT:
                    reduce_ada(6 + RED_OUT[s], RED_OUT[s], s % 4)
                unit_mms([s % 4], [s % 4], GH_, GL_, TOK, (g_hi, g_done, 0) if s == 0 else None)
            norm(1, TOK)
            norm_inverse(1, TOK)

            def mlp(layer, phase, tok, norm_no):
                with pe.Fori(0, CHUNKS) as i:
                    for s in range(2 * KT):
                        if s == 1:
                            continue
                        if layer == 0 and s in RED_MLP:
                            wait_slot(phase, i, s)
                            reduce_ada(i * 3 + 8 + RED_MLP[s], RED_MLP[s], s % 4)
                        if s == 0:
                            wait_unit(phase, i, 1)
                            wait_slot(phase, i, 1)
                            unit_mms([0, 1], [0, 1], HH, HL, tok, (h_hi, h_done, norm_no * KT))
                        else:
                            wait_unit(phase, i, s)
                            wait_slot(phase, i, s)
                            if s < KT:
                                unit_mms([s % 4], [s % 4], HH, HL, tok)
                            elif s == KT:
                                unit_mms([s % 4], [s % 4], GH_, GL_, tok,
                                         (g_hi, g_done, KT + layer * CHUNKS * KT + i * KT))
                            else:
                                unit_mms([s % 4], [s % 4], GH_, GL_, tok)

            mlp(0, "mlp0", TOK, 1)
            norm(2, TOK)
            norm_inverse(2, TOK)

            def scores(g, n):
                pair, j, item = item_pair(g, n), n % 4, 8 * g + n
                loc = ROWS * WIDTH[j]
                if j == 0:
                    pe.wait_ge(part_done, PARTS_FIRST // 2 if pair == 0 else
                               part_count(g, 2) if pair % 2 else part_count(g - 1, 5))
                if item >= 2:
                    pe.wait_ge(e_done, item - 1)
                for hh in range(2):
                    bank = PSB[:, 2 * (n % 2) + hh, :]
                    rows = slice(64 * hh, 64 * hh + 64)
                    pe.matmul(bank[:, 0:loc], SELR[rows, :],
                              free(MSKR[rows, MASK_OF[j], 0:WIDTH[j]], [[1, WIDTH[j]], [0, ROWS]]),
                              start=True, stop=False, skip_group_check=True)
                    for p_, (qt, kt) in enumerate(((QH, KH), (QH, KL), (QL, KH))):
                        q = qt[rows, pair % 2, P * j:P * (j + 1)]
                        at_ = 0
                        for a, b in KEYS[j]:
                            pe.matmul(bank[:, at_:at_ + b - a], q, kt[rows, pair % 2, a:b], start=False, stop=False,
                                      skip_group_check=True)
                            at_ += b - a
                        mm = pe.matmul(bank[:, loc:loc + CTX], q, kt[rows, pair % 2, LAT:TOK],
                                       start=False, stop=(p_ == 2), skip_group_check=True)
                mm.then_inc(s_mm, 1)

            def transposes(g, n):
                j, item = n % 4, 8 * g + n
                pe.wait_ge(p_done, item + 1)
                if item >= 1:
                    pe.wait_ge(pt_done, item)
                for t in range(4):
                    for hh in range(2):
                        first = KEY_TILES[j][t][3] if t < 2 else ROWS * WIDTH[j] + (t - 2) * P
                        mm = pe.transpose(PS[:, 2, (2 * t + hh) * P:(2 * t + hh + 1) * P],
                                          EE[:, n % 2, hh, first:first + P], IDN)
                mm.then_inc(pt_mm, 1)

            def values(g, n):
                j, item = n % 4, 8 * g + n
                pe.wait_ge(pt_done, item + 1)
                if item >= 1:
                    pe.wait_ge(o_done, item)
                tiles = [kt[:3] for kt in KEY_TILES[j]] + [(4, 0, P), (5, 0, P)]
                for t, (vt, r0, r1) in enumerate(tiles):
                    for p_, (a, b) in enumerate(((VH, PTH), (VH, PTL), (VL, PTH))):
                        mm = pe.matmul(PSB[:, 6, 0:2 * P],
                                       a[g % 2][vt // 2][r0:r1, vt % 2, n // 4 * P:(n // 4 + 1) * P], b[r0:r1, t, :],
                                       start=(t == 0 and p_ == 0), stop=(t == 3 and p_ == 2), skip_group_check=True)
                mm.then_inc(o_mm, 1)

            def qk_parts(parts_, ready=None):
                for k in range(KT):
                    for p_ in range(3):
                        wt, rt = ((WH, HH), (WL, HH), (WH, HL))[p_]
                        if ready and p_ != 1:
                            pe.wait_ge(ready[p_ // 2], ready[2] + k + 1)
                        for bank, ws, a, b in parts_:
                            mm = pe.matmul(PSB[:, bank, 0:b - a], wt[:, ws, k, :], rt[:, k, a:b],
                                           start=(k == 0 and p_ == 0), stop=(k == KT - 1 and p_ == 2))
                            if k == KT - 1 and p_ == 2:
                                mm.then_inc(part_mm, 1)

            def v_part(bank, ws, third):
                for t in range(2):
                    tt = 2 * third + t
                    for k in range(KT):
                        for p_, (ht, wt) in enumerate(((HH, WH), (HL, WH), (HH, WL))):
                            mm = pe.matmul(PSB[:, bank, t * 2 * P:(t + 1) * 2 * P], ht[:, k, tt * P:(tt + 1) * P],
                                           wt[:, ws:ws + 2, k, :], start=(k == 0 and p_ == 0),
                                           stop=(k == KT - 1 and p_ == 2), skip_group_check=True)
                mm.then_inc(part_mm, 1)

            def part(g, what, which, count):
                u = 4 + 6 * g + {"q": 2 * which - 2, "k_lat": 2 * which - 1, "k_ctx": 2 * which - 1, "v": 4}[what]
                wait_unit("attn", 0, u + (what == "v"))
                pe.wait_ge(part_done, count)
                if what == "v":
                    v_part(7, u % 4, which)
                else:
                    a, b = {"q": (0, LAT), "k_lat": (0, LAT), "k_ctx": (LAT, TOK)}[what]
                    qk_parts([(7, u % 4, a, b)])

            pe.wait_ge(sel_set, 2)
            pe.wait_ge(dve_evac, PRO + (3 + CHUNKS) * KT)
            wait_unit("attn", 0, 1)
            qk_parts([(0, 0, 0, LAT), (2, 1, 0, LAT), (3, 1, LAT, TOK)], (h_hi, h_done, 2 * KT))
            wait_unit("attn", 0, 3)
            v_part(4, 2, 0)
            scores(0, 0)
            v_part(5, 2, 1)
            scores(0, 1)
            v_part(6, 2, 2)
            for g in range(GROUPS):
                for n in range(8):
                    ahead = parts(g, n)
                    if n == 0:
                        pe.wait_ge(part_done, part_count(g, 0))
                    transposes(g, n)
                    if ahead:
                        part(g, *ahead[0], part_count(g, n))
                    values(g, n)
                    if 8 * g + n + 2 < 8 * GROUPS:
                        scores(*divmod(8 * g + n + 2, 8))
                    if len(ahead) > 1:
                        part(g, *ahead[1], part_count(g, n) + 1)
                    if g == GROUPS - 1 and n == 1:
                        pe.wait_ge(part_mm, PARTS_ALL)
                        pe.nop().then_inc(units_done, U_ATTN_OUT - U_ATTN)
            for s in range(KT):
                wait_unit("attn_out", 0, s)
                if s == 0:
                    pe.wait_ge(e_done, 8 * GROUPS)
                    pe.wait_ge(part_done, PARTS_ALL)
                    pe.wait_ge(o_done, 8 * GROUPS)
                if s >= 4:
                    wait_slot("attn_out", 0, s)
                unit_mms([s % 4], [s % 4], OH, OL, LAT)
            norm(3, LAT)
            norm_inverse(3, LAT)
            mlp(1, "mlp1", LAT, 3)
            norm(4, LAT)
            norm_inverse(4, LAT)
            for k in range(KT):
                pe.wait_ge(y_out, k + 1)
                if k >= 2:
                    pe.wait_ge(row_done, k - 1)
                for t in range(LAT // P):
                    mm = pe.transpose(PS[:, k % 2, t * P:(t + 1) * P], HF[:, k % 2, t * P:(t + 1) * P], IDN)
                mm.then_inc(yt_mm, 1)

        @block.scalar
        def _(act):
            for r, src in ((40, conv_w[0].rearrange("j (k p) -> (j k) p", p=P)),
                           (64, c.rearrange("b (k p) -> (b k) p", p=P)), (72, c_ctx.rearrange("(k p) -> k p", p=P))):
                act.dma_start(PRA[r:r + src.shape[0], :], src).then_inc(pa_in, 16)
            act.dma_start(CO[:, :], consts[:, 0:NCONST]).then_inc(const_in, 16)
            for t in range(1, TOK // P, 2):
                src = x[0, t * P:(t + 1) * P, :] if t < 4 else ctx[0, (t - 4) * P:(t - 3) * P, :]
                act.dma_start(XN[:, t, :], src).then_inc(x_in[t], 16)
            for k in range(1, KT, 2):
                act.dma_start(ADAF[:, k, :], ada_w[0, k * P:(k + 1) * P, 0:2 * D]).then_inc(af_in[k], 16)
            act.dma_start(FOLD[:, :], consts[:, NCONST:NCONST + P]).then_inc(fold_in, 16)

            def split_hi(u, slot, used=None):
                act.wait_ge(w_in[slot % 2], 16 * u[1] + 16)
                if used:
                    act.wait_ge(part_mm, used)
                else:
                    act.wait_ge(units_done, u[0] + PRO - 3)
                act.activation(WH[:, slot, :, :], WR[:, slot % 2, :, :], ACT.Copy).then_inc(hi_done, 1)

            def split_ahead(phase, i, s):
                u = unit_index(phase, i, s + 2)
                half = {"conv_in": i * 6, "conv_out": U_CONV_OUT // 2, "mlp0": U_MLP[0] // 2 + i * 8,
                        "attn": U_ATTN // 2 + i * 6, "attn_out": U_ATTN_OUT // 2,
                        "mlp1": U_MLP[1] // 2 + i * 8}[phase] + (s + 2) // 2
                split_hi((u, half), (s + 2) % 4)

            def squares(n, k, wait, tok):
                act.wait_ge(*wait)
                if k >= 3:
                    act.wait_ge(ss_done, 6 * n + k - 2)
                dst = SS if k == 0 else SQ[:, k % 2, :]
                ins = act.activation(dst[:, 0:LAT], XL[:, k, :], ACT.Square)
                if tok > LAT:
                    ins = act.activation(dst[:, LAT:TOK], XC[:, k, :], ACT.Square)
                ins.then_inc(sq_done, 1)

            def root(n, tok):
                for g, (a, b) in enumerate(SEG[tok]):
                    act.wait_ge(ms_done, norm_count(n) + g + 1)
                    act.activation(RMS[:, 0, a // P:b // P], PS[:, 2, g * 512 + a // P:g * 512 + b // P], ACT.Sqrt,
                                   bias=EPSC[:, 0:1], scale=1.0 / D).then_inc(rms_done, 1)

            def norm(n, tok, ada):
                if ada is not None:
                    act.wait_ge(am_set, 2 * (n + 1))
                for k in range(KT):
                    act.wait_ge(t1_done, n * KT + k + 1)
                    if ada is None:
                        if k >= 2:
                            act.wait_ge(yt_mm, k - 1)
                        act.activation(HF[:, k % 2, 0:LAT], T1[:, k % 2, 0:LAT], ACT.Copy,
                                       scale=PT_[:, 32 + k:33 + k]).then_inc(y_out, 1)
                        continue
                    layer, sh = ada
                    if k >= 2:
                        act.wait_ge(h_done, n * KT + k - 1)
                    for cond, (a, b) in enumerate(SEG[tok]):
                        ins = act.activation(HH[:, k, a:b], T1[:, k % 2, a:b], ACT.Identity,
                                             bias=ADA[:, layer, cond, sh + k:sh + k + 1], scale=AM[:, n, cond, k:k + 1])
                    ins.then_inc(h_hi, 1)
                    act.activation(HF[:, k % 2, 0:LAT], T1[:, k % 2, 0:LAT], ACT.Identity,
                                   bias=ADA[:, layer, 0, sh + k:sh + k + 1], scale=AM[:, n, 0, k:k + 1]).then_inc(hf_lat, 1)

            act.wait_ge(ones_set, 2)
            act.wait_ge(par_t, 1)
            act.activation(PT_[:, 0:80], PS[:, 3, 0:80], ACT.Copy).then_inc(act_evac, 1)
            act.wait_ge(par_t, 2)
            act.activation(PT_[:, 80:176], PS[:, 3, 512:608], ACT.Copy).then_inc(act_evac, 1)
            act.wait_ge(act_evac, 2)
            act.activation(CT[:, 0, :], PT_[:, 64:80], ACT.Exp, scale=-1.0).then_inc(silu_e, 1)
            act.wait_ge(const_in, 16)
            act.activation(SELR[:, :], CO[:, P:2 * P], ACT.Copy).then_inc(sel_set, 1)
            act.activation(MSKR[:, :, :], CO[:, 2 * P:].rearrange("p (m c) -> p m c", m=3), ACT.Copy).then_inc(sel_set, 1)
            for k in range(KT):
                squares(0, k, (dve_evac, k + 1), TOK)
            split_hi((0, 0), 0)
            split_hi((1, 0), 1)
            root(0, TOK)
            for n in range(2):
                act.wait_ge(af_mm, 2 * n + 2)
                act.activation(AROW[:, 2 * n:2 * n + 2, :], PSB[0:2, 2 * n:2 * n + 2, :], ACT.Copy).then_inc(af_rows, 1)
            norm(0, TOK, (0, 0))

            with act.Fori(0, 2) as i:
                for s in range(12):
                    split_ahead("conv_in", i, s)
                    t = s // 3
                    if s % 3 == 0:
                        act.wait_ge(units_done, PRO + 12 * i + s + 1)
                        act.activation(CS_[:, t % 2, :], PS[:, s % 4, 0:TOK], ACT.Copy).then_inc(act_evac, 1)
                    elif s % 3 == 1:
                        act.wait_ge(dve_evac, PRO + 8 * i + 2 * t + 1)
                        act.activation(YY[:, t % 2, 0:TOK + 1], UU[:, t % 2, 0:TOK + 1], ACT.Copy,
                                       scale=PT_[:, bass.ds(i * 4 + 40 + t, 1)]).then_inc(y_done, 1)
                    else:
                        act.wait_ge(dve_evac, PRO + 8 * i + 2 * t + 2)
                        act.activation(GH_[:, bass.ds(i * 4 + t, 1), :].rearrange("p a n -> p (a n)"),
                                       GF[:, t % 2, :], ACT.Copy).then_inc(g_hi, 1)
            for s in range(KT):
                split_ahead("conv_out", 0, s)
                squares(1, s, (dve_evac, PRO + 2 * KT + s + 1), TOK)
            root(1, TOK)
            norm(1, TOK, (0, 24))

            def mlp(layer, phase, tok, norm_next):
                tiles = KT + layer * CHUNKS * KT

                def chunk(i, last):
                    for s in range(2 * KT):
                        if not (last and layer == 1 and s >= 2 * KT - 2):
                            split_ahead(phase, i, s)
                        if s < KT:
                            act.wait_ge(units_done, unit_index(phase, i, s) + PRO + 1)
                            act.wait_ge(a_done, i * KT + layer * CHUNKS * KT + s + 1)
                            act.activation(RR[:, s % 2, 0:tok], PS[:, s % 4, 0:tok], ACT.Relu).then_inc(act_evac, 1)
                            act.wait_ge(act_evac, evac_counts(phase, i, s + 1)[0])
                            act.activation(GH_[:, s, 0:tok], RR[:, s % 2, 0:tok], ACT.Square).then_inc(g_hi, 1)
                        elif last:
                            squares(norm_next, s - KT, (dve_evac, evac_counts(phase, i, s + 1)[1]), tok)

                with act.Fori(0, CHUNKS - 1) as i:
                    chunk(i, False)
                chunk(CHUNKS - 1, True)

            def split_attn(u):
                split_hi((U_ATTN + u, (U_ATTN + u) // 2), u % 4, parts_of_unit(u - 4) if u >= 4 else None)

            mlp(0, "mlp0", TOK, 2)
            root(2, TOK)
            split_attn(2)
            norm(2, TOK, (1, 0))
            split_attn(3)

            def exps(g, n):
                keys = ROWS * WIDTH[n % 4] + CTX
                act.wait_ge(m_neg, 8 * g + n + 1)
                for hh in range(2):
                    ins = act.activation(EE[:, n % 2, hh, 0:keys], PSB[:, 2 * (n % 2) + hh, 0:keys], ACT.Exp,
                                         bias=SM[:, n % 2, 2, hh:hh + 1], accum_out=SM[:, n % 2, 3, hh:hh + 1])
                ins.then_inc(e_done, 1)

            def take_hi(what, which, g, count, bank):
                act.wait_ge(part_mm, count)
                if what == "v":
                    if g >= 2:
                        act.wait_ge(o_mm, 8 * (g - 1))
                    act.activation(VH[g % 2][which][:, :, :], PSB[:, bank, :].rearrange("p (t n) -> p t n", t=2),
                                   ACT.Copy).then_inc(part_hi, 1)
                    return
                if which >= 2:
                    act.wait_ge(s_mm, 4 * (which - 1))
                if what == "q":
                    for a, b, to in Q_ORDER:
                        ins = act.activation(QH[:, which % 2, to:to + b - a], PSB[:, bank, a:b], ACT.Copy, scale=ATTN_SCALE)
                    ins.then_inc(part_hi, 1)
                else:
                    a, b = (0, LAT) if what == "k_lat" else (LAT, TOK)
                    act.activation(KH[:, which % 2, a:b], PSB[:, bank, 0:b - a], ACT.Copy).then_inc(part_hi, 1)

            take_hi("q", 0, 0, 1, 0)
            take_hi("k_lat", 0, 0, 2, 2)
            take_hi("k_ctx", 0, 0, 3, 3)
            split_attn(4)
            take_hi("v", 0, 0, 4, 4)
            exps(0, 0)
            split_attn(5)
            take_hi("v", 1, 0, 5, 5)
            take_hi("v", 2, 0, 6, 6)
            for g in range(GROUPS):
                for n in range(8):
                    item = 8 * g + n
                    act.wait_ge(pt_mm, item + 1)
                    act.activation(PTH[:, :, :].rearrange("p t n -> p (t n)"), PS[:, 2, :], ACT.Copy).then_inc(pt_hi, 1)
                    if item + 1 < 8 * GROUPS:
                        exps(*divmod(item + 1, 8))
                    ahead = parts(g, n)
                    if n < 4 and g < GROUPS - 1:
                        split_attn(6 + 6 * g + n)
                    elif n in (4, 5):
                        split_attn(4 + 6 * (g + 1) + n - 4 if g < GROUPS - 1 else U_ATTN_OUT - U_ATTN + n - 4)
                    if ahead:
                        what, which = ahead[0]
                        take_hi(what, which + (0 if what == "v" else 2 * g), g + 1, part_count(g, n) + 1, 7)
                    act.wait_ge(o_mm, item + 1)
                    for hh in range(2):
                        rows = slice(64 * hh, 64 * hh + 64)
                        ins = act.activation(OH[rows, item_pair(g, n), P * (n % 4):P * (n % 4 + 1)],
                                             PSB[rows, 6, hh * P:(hh + 1) * P], ACT.Copy)
                    ins.then_inc(o_hi, 1)
                    if len(ahead) > 1:
                        take_hi(ahead[1][0], ahead[1][1] + 2 * g, g + 1, part_count(g, n) + 2, 7)
            for s in range(KT):
                split_ahead("attn_out", 0, s)
                squares(3, s, (dve_evac, PRO + (3 + CHUNKS) * KT + s + 1), LAT)
            root(3, LAT)
            norm(3, LAT, (1, 24))
            mlp(1, "mlp1", LAT, 4)
            root(4, LAT)
            norm(4, LAT, None)

        @block.vector
        def _(dve):
            def split_lo(u, slot):
                dve.wait_ge(hi_done, u + 1)
                dve.tensor_tensor(WL[:, slot, :, :], WR[:, slot % 2, :, :], WH[:, slot, :, :].bitcast(F32),
                                  ALU.subtract).then_inc(lo_done, 1)

            def split_attn(u):
                split_lo(U_ATTN + u, u % 4)

            def split_ahead(phase, i, s):
                split_lo(unit_index(phase, i, s + 2), (s + 2) % 4)

            def sums(n, k, tok):
                if k == 0 or k == KT - 1:
                    return
                dve.wait_ge(sq_done, n * KT + k + 1)
                if k >= 2:
                    dve.wait_ge(ss_done, 6 * n + k - 1)
                dve.tensor_tensor(SS[:, 0:tok], SS[:, 0:tok], SQ[:, k % 2, 0:tok], ALU.add).then_inc(ss_done, 1)

            def norm(n, tok, ada, meanwhile=None):
                for g, (a, b) in enumerate(SEG[tok]):
                    t0, t1_ = a // P, b // P
                    dve.wait_ge(rms_done, norm_count(n) + g + 1)
                    dve.reciprocal(RMS[:, 1, t0:t1_], RMS[:, 0, t0:t1_]).then_inc(rec_done, 1)
                    dve.wait_ge(rec_done, norm_count(n) + g + 1)
                    dve.tensor_tensor(DI[:, t0:t1_, :], free(IDN, [[0, t1_ - t0], [1, P]]),
                                      free(RMS[:, 1, t0:t1_], [[1, t1_ - t0], [0, P]]), ALU.mult).then_inc(diag_done, 1)
                if meanwhile:
                    meanwhile()

                def t1(k):
                    if ada is None and k >= 2:
                        dve.wait_ge(y_out, k - 1)
                    elif k >= 2:
                        dve.wait_ge(hf_lat, n * KT + k - 1)
                    if k == 0:
                        dve.wait_ge(inv_done, norm_count(n) + 1)
                    if n == 2:
                        for a, dims in ((0, [[COLS - 8, 2], [1, 8], [COLS, ROWS]]), (8, [[1, COLS - 16], [COLS, ROWS]])):
                            ins = dve.tensor_tensor(T1[:, k % 2, a * WIN:a * WIN + ROWS * (16 if a == 0 else COLS - 16)],
                                                    free(XL[:, k, a:a + 1], dims), free(PS[:, 3, a:a + 1], dims), ALU.mult)
                    else:
                        ins = dve.tensor_tensor(T1[:, k % 2, 0:LAT], XL[:, k, :], PS[:, 3, 0:LAT], ALU.mult)
                    if tok > LAT:
                        if k == 0:
                            dve.wait_ge(inv_done, norm_count(n) + 2)
                        ins = dve.tensor_tensor(T1[:, k % 2, LAT:TOK], XC[:, k, :], PS[:, 3, LAT:TOK], ALU.mult)
                    ins.then_inc(t1_done, 1)

                t1(0)
                for k in range(KT):
                    if ada is None:
                        if k + 1 < KT:
                            t1(k + 1)
                        dve.wait_ge(yt_mm, k + 1)
                        dve.tensor_copy(OUTB[:, k, :, :].rearrange("p t n -> p (t n)"), PS[:, k % 2, 0:LAT])\
                            .then_inc(row_done, 1)
                        continue
                    layer, sh = ada
                    if tok > LAT:
                        dve.wait_ge(t1_done, n * KT + k + 1)
                        dve.tensor_scalar(HF[:, k % 2, LAT:TOK], T1[:, k % 2, LAT:TOK], AM[:, n, 1, k:k + 1],
                                          ADA[:, layer, 1, sh + k:sh + k + 1], ALU.mult, ALU.add).then_inc(hf_ctx, 1)
                    if k + 1 < KT:
                        t1(k + 1)
                    if tok > LAT:
                        dve.wait_ge(hf_ctx, n * KT + k + 1)
                    dve.wait_ge(h_hi, n * KT + k + 1)
                    dve.wait_ge(hf_lat, n * KT + k + 1)
                    dve.tensor_tensor(HL[:, k, 0:tok], HF[:, k % 2, 0:tok], HH[:, k, 0:tok].bitcast(F32),
                                      ALU.subtract).then_inc(h_done, 1)

            def scale_terms(n, layer, gcol, sc, count):
                dve.wait_ge(ada_set, count)
                for cond in range(2):
                    dve.scalar_tensor_tensor(AM[:, n, cond, :], ADA[:, layer, cond, sc:sc + KT], 1.0,
                                             PT_[:, gcol:gcol + KT], ALU.add, ALU.mult).then_inc(am_set, 1)

            def ada_entry(layer, block_, b, q, half, slot):
                entry = block_ * 4 + q
                dve.wait_ge(a_in[slot], 16 * half + 16)
                for kk in range(2):
                    for cond in range(2):
                        sc = CSI[:, 2 * q + kk, cond:cond + 1]
                        a = AC[:, cond, :]
                        first = q == 0 and kk == 0
                        if kk:
                            dve.wait_ge(ada_step, entry * 3 + cond + 1)
                        elif not first:
                            dve.wait_ge(*((ada_used, entry + 2) if cond else (ada_step, entry * 3)))
                        if first:
                            ins = dve.tensor_scalar(a, AR[:, slot, kk, :], sc, None, ALU.mult)
                        else:
                            ins = dve.scalar_tensor_tensor(a, AR[:, slot, kk, :], sc, a, ALU.mult, ALU.add)
                        ins.then_inc(ada_used if kk and cond else ada_step, 1)
                if q == 3:
                    dve.wait_ge(ada_step, entry * 3 + 3)
                    dve.wait_ge(ada_used, entry + 3)
                    dve.transpose(AT[:, :, :].rearrange("p c n -> p (c n)"), AC[:, :, :].rearrange("p c n -> p (c n)"))\
                        .then_inc(ada_turned, 1)
                    dve.wait_ge(ada_turned, block_ + 1)
                    dve.wait_ge(ada_red, block_ + 4)
                    dve.reduce_sum(AQ[:, b, :], AT[:, :, :].rearrange("p c (j n) -> p (c j) n", n=32), AX_X)\
                        .then_inc(ada_part, 1)

            def ada_out(layer, slot, tile):
                for a in range(4):
                    rows = slice(32 * a, 32 * a + 32)
                    dve.tensor_tensor(ADA[rows, layer, :, bass.ds(tile, 4)],
                                      free(PS[rows, slot, TOK + a:TOK + a + 1], [[16, 2], [4, 4]]),
                                      PT_[rows, bass.ds(tile + 80 + 48 * layer, 4)].rearrange("p (c t) -> p c t", c=1)
                                      .to_broadcast([32, 2, 4]), ALU.add).then_inc(ada_set, 1)

            def residual(slot, k, layer, gate, tok, by_column=False):
                y, xk = PS[:, slot, 0:LAT], XL[:, k, :]
                if by_column:
                    y = y.rearrange("p (c r) -> p r c", r=ROWS)
                    xk = xk.rearrange("p (r c) -> p r c", r=ROWS)
                ins = dve.scalar_tensor_tensor(xk, y, ADA[:, layer, 0, gate + k:gate + k + 1], xk, ALU.mult, ALU.add)
                if tok > LAT:
                    ins = dve.scalar_tensor_tensor(XC[:, k, :], PS[:, slot, LAT:TOK],
                                                   ADA[:, layer, 1, gate + k:gate + k + 1], XC[:, k, :], ALU.mult, ALU.add)
                ins.then_inc(dve_evac, 1)

            for what in (lo_done, lo_done, ada_used, ada_used, a_done, a_done):
                dve.engine_nop().then_inc(what, 1)
            for k in range(KT):
                dve.wait_ge(units_done, k + 1)
                dve.tensor_copy(XL[:, k, :], PS[:, k % 4, 0:LAT])
                dve.tensor_copy(XC[:, k, :], PS[:, k % 4, LAT:TOK]).then_inc(dve_evac, 1)
                if k == 1:
                    dve.wait_ge(silu_e, 1)
                    dve.tensor_scalar(CT[:, 1, :], CT[:, 0, :], 1.0, None, ALU.add).then_inc(silu_d, 1)
                    dve.wait_ge(silu_d, 1)
                    dve.reciprocal(CT[:, 2, :], CT[:, 1, :]).then_inc(silu_r, 1)
                    dve.wait_ge(silu_r, 1)
                    dve.tensor_tensor(CSI[:, :, :], PT_[:, 64:80].rearrange("p (a k) -> p k a", a=2),
                                      CT[:, 2, :].rearrange("p (a k) -> p k a", a=2), ALU.mult).then_inc(silu_done, 1)
                if k == 3:
                    dve.wait_ge(rpb_zero, 1)
                    dve.wait_ge(rpb_in, 16)
                    dve.tensor_copy(free(RPB[:, 711:712], [[-BPITCH, 15], [-1, 31]]), RPN[:, :, :]).then_inc(rpb_rev, 1)
                if k >= 1:
                    sums(0, k - 1, TOK)
            sums(0, KT - 1, TOK)
            split_lo(0, 0)
            split_lo(1, 1)

            def first_ada():
                dve.wait_ge(ada_red, 6)
                for cond in range(2):
                    dve.tensor_tensor(ADA[:, 0, cond, 0:16], free(PS[:, 2, cond:cond + 1], [[2, 16]]), PT_[:, 80:96],
                                      ALU.add).then_inc(ada_set, 1)
                scale_terms(0, 0, 0, 8, 2)

            dve.wait_ge(scratch_in, 16)
            norm(0, TOK, (0, 0), first_ada)

            dve.wait_ge(h_done, KT)
            for col in (0, LAT + 1, TOK + 2):
                dve.memset(UU[:, :, col:col + 1], 0.0)
            with dve.Fori(0, 2) as i:
                n = 0
                for s in range(12):
                    split_ahead("conv_in", i, s)
                    for b, q in ADA_CONV[s]:
                        ada_entry(0, i * 3 + b, b, q, i * 6 + n // 2, n % 2)
                        n += 1
                    t = s // 3
                    if s % 3:
                        dve.wait_ge(units_done, PRO + 12 * i + s + 1)
                        if s in RED_CONV:
                            ada_out(0, s % 4, (i * 3 + 4 + RED_CONV[s]) * 4)
                    if s % 3 == 1:
                        if t:
                            dve.wait_ge(g_done, 4 * i + t)
                        dve.wait_ge(act_evac, evac_counts("conv_in", i, s)[0])
                        dve.tensor_tensor(UU[:, t % 2, 1:LAT + 1], PS[:, s % 4, 0:LAT], CS_[:, t % 2, 0:LAT], ALU.mult)
                        dve.tensor_tensor(UU[:, t % 2, LAT + 2:TOK + 2], PS[:, s % 4, LAT:TOK], CS_[:, t % 2, LAT:TOK],
                                          ALU.mult).then_inc(dve_evac, 1)
                    elif s % 3 == 2:
                        y = YY[:, t % 2, 0:TOK + 1]
                        dve.wait_ge(y_done, 4 * i + t + 1)
                        for tap in (1, 2):
                            dve.scalar_tensor_tensor(y, UU[:, t % 2, tap:tap + TOK + 1],
                                                     PT_[:, bass.ds(i * 4 + 40 + KT * tap + t, 1)], y,
                                                     ALU.mult, ALU.add).then_inc(y_mid, 1)
                            dve.wait_ge(y_mid, 8 * i + 2 * t + tap)
                        dve.tensor_tensor(GF[:, t % 2, 0:LAT], PS[:, s % 4, 0:LAT], YY[:, t % 2, 0:LAT], ALU.mult)
                        dve.tensor_tensor(GF[:, t % 2, LAT:TOK], PS[:, s % 4, LAT:TOK], YY[:, t % 2, LAT + 1:TOK + 1],
                                          ALU.mult).then_inc(dve_evac, 1)
                        dve.wait_ge(g_hi, 4 * i + t + 1)
                        hi = GH_[:, bass.ds(i * 4 + t, 1), :].bitcast(F32).rearrange("p a n -> p (a n)")
                        dve.tensor_tensor(GL_[:, bass.ds(i * 4 + t, 1), :].rearrange("p a n -> p (a n)"),
                                          GF[:, t % 2, :], hi, ALU.subtract).then_inc(g_done, 1)
            scale_terms(1, 0, 16, 32, 26)
            n = 0
            for s in range(KT):
                split_ahead("conv_out", 0, s)
                for b, q in ADA_OUT[s]:
                    ada_entry(0, 6 + b, b, q, 12 + n // 2, n % 2)
                    n += 1
                dve.wait_ge(units_done, PRO + U_CONV_OUT + s + 1)
                if s in RED_OUT:
                    ada_out(0, s % 4, (10 + RED_OUT[s]) * 4)
                residual(s % 4, s, 0, 16, TOK)
                if s:
                    sums(1, s - 1, TOK)
            sums(1, KT - 1, TOK)
            dve.wait_ge(ada_set, 34)
            norm(1, TOK, (0, 24))

            def mlp(layer, phase, tok, norm_next):
                tiles = layer * CHUNKS * KT

                def chunk(i, last):
                    n = 0
                    for s in range(2 * KT):
                        if not (last and layer == 1 and s >= 2 * KT - 2):
                            split_ahead(phase, i, s)
                        if layer == 0:
                            for b, q in ADA_MLP[s]:
                                ada_entry(1, i * 3 + 8 + b, b, q, i * 6 + 16 + n // 2, n % 2)
                                n += 1
                        if s < KT:
                            dve.wait_ge(act_evac, evac_counts(phase, i, s + 1)[0])
                            dve.wait_ge(g_done, i * KT + KT + tiles + s - 1)
                            r = RR[:, s % 2, 0:tok]
                            dve.tensor_tensor(AA[:, s % 2, 0:tok], r, r, ALU.mult).then_inc(a_done, 1)
                            dve.wait_ge(a_done, i * KT + 2 + tiles + s + 1)
                            dve.wait_ge(g_hi, i * KT + KT + tiles + s + 1)
                            dve.tensor_tensor(GL_[:, s, 0:tok], AA[:, s % 2, 0:tok], GH_[:, s, 0:tok].bitcast(F32),
                                              ALU.subtract).then_inc(g_done, 1)
                        else:
                            dve.wait_ge(units_done, unit_index(phase, i, s) + PRO + 1)
                            if layer == 0 and s in RED_MLP:
                                ada_out(1, s % 4, (i * 3 + RED_MLP[s]) * 4)
                            residual(s % 4, s - KT, layer, 40, tok)
                            if last and s > KT:
                                sums(norm_next, s - KT - 1, tok)

                with dve.Fori(0, CHUNKS - 1) as i:
                    chunk(i, False)
                chunk(CHUNKS - 1, True)
                sums(norm_next, KT - 1, tok)

            mlp(0, "mlp0", TOK, 2)
            scale_terms(2, 1, KT, 8, 82)
            scale_terms(3, 1, 3 * KT, 32, 82)
            norm(2, TOK, (1, 0), lambda: split_attn(2))
            split_attn(3)

            def maxima(g, n):
                wide, pair, item = WIDTH[n % 4], item_pair(g, n), 8 * g + n
                loc = ROWS * wide
                b0 = 2 * (n % 2)
                if n % 4 == 0:
                    dve.wait_ge(bias_in[pair % 2], 16 * (pair // 2 + 1))
                dve.wait_ge(s_mm, item + 1)
                dve.reduce_max(SM[:, n % 2, 0, :], PSB[:, b0:b0 + 2, loc:loc + CTX], AX_X,
                               negate=True).then_inc(m_ctx, 1)
                for hh in range(2):
                    s_loc = PSB[:, b0 + hh, 0:loc].rearrange("p (c r) -> p c r", r=ROWS)
                    last = BRUN - 1 - (8 if n % 4 == 0 else 0)
                    bias = free(BT[:, pair % 2, hh, last:last + 1], [[-1, wide], [-BPITCH, ROWS]])
                    dve.tensor_tensor_reduce(s_loc, s_loc, bias, 1.0, LOWEST, ALU.add,
                                             ALU.max, SM[:, n % 2, 1, hh:hh + 1]).then_inc(m_all, 1)
                dve.wait_ge(m_all, 2 * item + 2)
                dve.wait_ge(m_ctx, item + 1)
                dve.scalar_tensor_tensor(SM[:, n % 2, 2, :], SM[:, n % 2, 1, :], -1.0, SM[:, n % 2, 0, :],
                                         ALU.mult, ALU.min).then_inc(m_neg, 1)

            def recip(g, n):
                dve.wait_ge(e_done, 8 * g + n + 1)
                dve.reciprocal(SM[:, n % 2, 4, :], SM[:, n % 2, 3, :]).then_inc(r_done, 1)

            def take_lo(what, which, g, count, bank):
                dve.wait_ge(part_hi, count)
                if what == "v":
                    dve.tensor_tensor(VL[g % 2][which][:, :, :], PSB[:, bank, :].rearrange("p (t n) -> p t n", t=2),
                                      VH[g % 2][which][:, :, :].bitcast(F32), ALU.subtract).then_inc(part_done, 1)
                elif what == "q":
                    for a, b, to in Q_ORDER:
                        ins = dve.scalar_tensor_tensor(
                            QL[:, which % 2, to:to + b - a], PSB[:, bank, a:b], ATTN_SCALE,
                            QH[:, which % 2, to:to + b - a].bitcast(F32), ALU.mult, ALU.subtract)
                    ins.then_inc(part_done, 1)
                else:
                    a, b = (0, LAT) if what == "k_lat" else (LAT, TOK)
                    dve.tensor_tensor(KL[:, which % 2, a:b], PSB[:, bank, 0:b - a], KH[:, which % 2, a:b].bitcast(F32),
                                      ALU.subtract).then_inc(part_done, 1)

            take_lo("q", 0, 0, 1, 0)
            take_lo("k_lat", 0, 0, 2, 2)
            take_lo("k_ctx", 0, 0, 3, 3)
            split_attn(4)
            take_lo("v", 0, 0, 4, 4)
            maxima(0, 0)
            recip(0, 0)
            split_attn(5)
            take_lo("v", 1, 0, 5, 5)
            take_lo("v", 2, 0, 6, 6)
            for g in range(GROUPS):
                for n in range(8):
                    item = 8 * g + n
                    if item + 1 < 8 * GROUPS:
                        maxima(*divmod(item + 1, 8))
                    dve.wait_ge(pt_hi, item + 1)
                    dve.tensor_tensor(PTL[:, :, :].rearrange("p t n -> p (t n)"), PS[:, 2, :],
                                      PTH[:, :, :].bitcast(F32).rearrange("p t n -> p (t n)"),
                                      ALU.subtract).then_inc(pt_done, 1)
                    if item + 1 < 8 * GROUPS:
                        recip(*divmod(item + 1, 8))
                    ahead = parts(g, n)
                    if n < 4 and g < GROUPS - 1:
                        split_attn(6 + 6 * g + n)
                    elif n in (4, 5):
                        split_attn(4 + 6 * (g + 1) + n - 4 if g < GROUPS - 1 else U_ATTN_OUT - U_ATTN + n - 4)
                    if ahead:
                        what, which = ahead[0]
                        take_lo(what, which + (0 if what == "v" else 2 * g), g + 1, part_count(g, n) + 1, 7)
                    dve.wait_ge(o_hi, item + 1)
                    for hh in range(2):
                        rows = slice(64 * hh, 64 * hh + 64)
                        cols = slice(P * (n % 4), P * (n % 4 + 1))
                        ins = dve.tensor_tensor(OL[rows, item_pair(g, n), cols], PSB[rows, 6, hh * P:(hh + 1) * P],
                                                OH[rows, item_pair(g, n), cols].bitcast(F32), ALU.subtract)
                    ins.then_inc(o_done, 1)
                    if len(ahead) > 1:
                        take_lo(ahead[1][0], ahead[1][1] + 2 * g, g + 1, part_count(g, n) + 2, 7)
            for s in range(KT):
                split_ahead("attn_out", 0, s)
                dve.wait_ge(units_done, PRO + U_ATTN_OUT + s + 1)
                residual(s % 4, s, 1, 16, LAT, by_column=True)
                if s:
                    sums(3, s - 1, LAT)
            sums(3, KT - 1, LAT)
            norm(3, LAT, (1, 24))
            mlp(1, "mlp1", LAT, 4)
            norm(4, LAT, None)


_INS = ["x", "c", "ctx", "c_ctx", "norm1_g", "norm2_g", "ada_w", "ada_b", "conv_in_w", "conv_w", "conv_out_w",
        "attn_qkv_w", "attn_rpb", "attn_out_w", "mlp_w1", "mlp_w2", "final_g"]
_OUTS = [((1, 512, 1024), "float32")]


def kernel(**inputs):
    import numpy as _np
    import concourse.bacc as _bacc
    from concourse import mybir as _mybir
    from concourse.bass_utils import run_bass_kernel_spmd as _run

    nc = _bacc.Bacc("TRN2", target_bir_lowering=False, num_devices=1)
    arrays, args = {}, []
    for name in _INS:
        a = _np.ascontiguousarray(inputs[name])
        arrays[f"in_{name}_dram"] = a
        args.append(nc.dram_tensor(f"in_{name}_dram", a.shape, _mybir.dt.from_np(a.dtype), kind="ExternalInput").ap())
    arrays["consts_dram"] = constants()
    args.append(nc.dram_tensor("consts_dram", (P, NCONST + P), _mybir.dt.float32, kind="ExternalInput").ap())
    for i, (shape, dtype) in enumerate(_OUTS):
        dt = _mybir.dt.from_np(_np.dtype(dtype))
        args.append(nc.dram_tensor(f"out_{i}_dram", shape, dt, kind="ExternalOutput").ap())
    build(nc, *args)
    r = _run(nc, [arrays], core_ids=[0])
    return r.results[0]["out_0_dram"]
```

```python
from contextlib import ExitStack

import numpy as np

import concourse.bass as bass
from concourse import mybir

F32 = mybir.dt.float32
F32R = mybir.dt.float32r
ALU = mybir.AluOpType
ACT = mybir.ActivationFunctionType
AX_X = mybir.AxisListType.X

P = 128
D = 1024
KT = D // P
LAT, CTX = 512, 256
TOK = LAT + CTX
ROWS, COLS = 8, 64
HEADS, DH = 16, 64
WIN = 16
F = 4 * D
CHUNKS = F // D
EPS = 1e-6
MASKED = -1e30
LOWEST = -3.0e38
ATTN_SCALE = DH ** -0.5

U_CONV_IN = 0
U_CONV_OUT = U_CONV_IN + 3 * KT
U_MLP = [U_CONV_OUT + KT, 0]
U_ATTN = U_MLP[0] + 2 * KT * CHUNKS
U_ATTN_OUT = U_ATTN + 3 * KT
U_MLP[1] = U_ATTN_OUT + KT
UNITS = U_MLP[1] + 2 * KT * CHUNKS
PRO = KT

WIDTH = [24, 32, 32, 24]
KEYS = [[(0, 64), (128, 256)], [(128, 384)], [(256, 512)], [(384, 512), (64, 128)]]
KEY_TILES = [
    [(0, 0, 64, 0), (1, 0, 128, 64)],
    [(1, 0, 128, 0), (2, 0, 128, 128)],
    [(2, 0, 128, 0), (3, 0, 128, 128)],
    [(3, 0, 128, 0), (0, 64, 128, 64)],
]
Q_ORDER = [(0, 64, 0), (128, 512, 64), (64, 128, 448)]
MASK_OF = [0, 1, 1, 2]
GROUPS = 4
PARTS = {0: [("q", 1)], 1: [("k_lat", 1), ("k_ctx", 1)], 2: [("q", 2)], 3: [("k_lat", 2)], 4: [("k_ctx", 2)],
         5: [("v", 0)], 6: [("v", 1)], 7: [("v", 2)]}
PARTS_FIRST, PARTS_GROUP = 6, 9
PARTS_ALL = PARTS_FIRST + PARTS_GROUP * (GROUPS - 1) + 3
UNIT_PARTS = [1, 3, 4, 6, 9, 9]
OUT_TILES = {0: ((), (0,)), 1: ((), ()), 2: ((1,), ()), 3: ((2,), ()), 4: ((3,), ()), 5: ((4,), ()), 6: ((5,), ()),
             7: ((6,), (7,))}
OUT_UNITS = [((0, 4, 0, 2), 2), ((4, 6, 0, 4), 4), ((0, 4, 2, 4), 4), ((0, 4, 4, 6), 6), ((4, 6, 4, 8), 8),
             ((0, 4, 6, 8), 8), ((6, 8, 0, 4), 12), ((6, 8, 4, 8), 16)]
OUT_OF = [[(0, 1), (2, 1), (3, 4), (5, 4)][c // 2] for c in range(8)]
OUT_ROWS = (0, 1, 3, 2)
OUT_SPLITS = {0: (0, 1), 1: (2,), 2: (3,), 3: (4,), 5: (5,), 6: (6,), 7: (7,)}
BPITCH = 47
BHEAD = 15 * BPITCH + 15
BRUN = ROWS * BPITCH


def constants():
    ident = np.eye(P, dtype=np.float32)
    sel = np.zeros((P, P), np.float32)
    mask = np.zeros((P, 3, 32), np.float32)
    for half in (0, 64):
        for qc in range(WIN):
            sel[half + qc, qc * ROWS:(qc + 1) * ROWS] = 1.0
            for m, start in enumerate((max(qc - 8, 0), qc, min(qc, 8))):
                mask[half + qc, m, :] = MASKED
                mask[half + qc, m, start:start + WIN] = 0.0
    return np.ascontiguousarray(np.concatenate(
        [ident, sel, mask.reshape(P, 96), np.tile(np.eye(32, dtype=np.float32), (4, 4))], axis=1))


NCONST = 2 * P + 96


def free(view, dims):
    return bass.AP(view.tensor, view.offset, [list(view.ap[0])] + dims)


def build(nc, x, c, ctx, c_ctx, norm1_g, norm2_g, ada_w, ada_b, conv_in_w, conv_w, conv_out_w,
          attn_qkv_w, attn_rpb, attn_out_w, mlp_w1, mlp_w2, final_g, consts, out):
    base = (nc.sbuf_base + 63) // 64 * 64

    def at(name, shape, dt, word):
        assert base + 4 * (word + int(np.prod(shape[1:]))) <= nc.sbuf_usable_end, name
        return nc.alloc_sbuf_tensor_at(name, shape, dt, offset=base + 4 * word)

    o_x = 0
    o_h = o_x + KT * TOK
    o_g = o_h + 2 * KT * TOK
    o_s = o_g + 2 * KT * TOK
    o_wr = o_s + 6400
    o_ar = o_wr + 2 * KT * P
    o_wh = o_ar + 2 * KT * P
    o_wl = o_wh + 4 * KT * P
    o_acc = o_wl + 4 * KT * P
    o_misc = o_acc + 2 * 2 * 512

    XL = at("x_latent", [P, KT, LAT], F32, o_x)
    XC = at("x_context", [P, KT, CTX], F32, o_x + KT * LAT)
    BT = at("bias_rows", [P, 2, 2, BRUN], F32, o_x + KT * LAT)
    HH = at("h_hi", [P, KT, TOK], F32R, o_h)
    HL = at("h_lo", [P, KT, TOK], F32R, o_h + KT * TOK)
    XN = at("x_rows", [P, TOK // P, D], F32, o_h)
    PRA = at("param_rows_a", [80, P], F32, o_h + KT * TOK)
    PRB = at("param_rows_b", [96, P], F32, o_h + KT * TOK + P)
    RPB = at("rpb_reversed", [HEADS, BHEAD], F32, o_h + KT * TOK + 2 * P)
    RPN = at("rpb_rows", [HEADS, 15, 31], F32, o_h + KT * TOK + 2 * P + BHEAD)
    XG = at("x_times_gain", [P, KT, LAT], F32, o_h)
    OUTB = at("out_rows", [P, LAT // P, D], F32, o_h + KT * TOK)
    GH_ = at("g_hi", [P, KT, TOK], F32R, o_g)
    GL_ = at("g_lo", [P, KT, TOK], F32R, o_g + KT * TOK)
    ADAF = at("ada_first", [P, KT, 2 * D], F32, o_g)
    OH = at("o_hi", [P, KT, LAT], F32R, o_g)
    OL = at("o_lo", [P, KT, LAT], F32R, o_g + KT * LAT)
    QH = at("q_hi", [P, 2, LAT], F32R, o_g + 2 * KT * LAT)
    QL = at("q_lo", [P, 2, LAT], F32R, o_g + 2 * KT * LAT + 2 * LAT)
    PTH = at("pt_hi", [P, 4, 2 * P], F32R, o_g + 2 * KT * LAT + 4 * LAT)
    PTL = at("pt_lo", [P, 4, 2 * P], F32R, o_g + 2 * KT * LAT + 4 * LAT + 8 * P)
    KH = at("k_hi", [P, 2, TOK], F32R, o_s)
    KL = at("k_lo", [P, 2, TOK], F32R, o_s + 2 * TOK)
    o_end = o_misc + NCONST + 2 * P + 96 + 496
    v_at = [[[o_s + 4 * TOK + 12 * P * part + 4 * P * b for b in range(3)] for part in range(2)],
            [[o_ar, o_ar + 4 * P, o_ar + 8 * P], [o_ar + 12 * P, o_x + KT * LAT + 4 * BRUN, o_end]]]
    VH, VL = ([[at(f"v_{what}{buf}_{b}", [P, 2, 2 * P], F32R, v_at[buf][part][b]) for b in range(3)]
               for buf in range(2)] for part, what in enumerate(("hi", "lo")))
    CS_ = at("conv_c", [P, 2, TOK], F32, o_s)
    UU = at("conv_u", [P, 2, TOK + 8], F32, o_s + 2 * TOK)
    YY = at("conv_y", [P, 2, TOK + 8], F32, o_s + 4 * TOK + 16)
    GF = at("conv_g", [P, 2, TOK], F32, o_s + 6 * TOK + 32)
    RR = at("relu", [P, 2, TOK], F32, o_s)
    AA = at("relu2", [P, 2, TOK], F32, o_s + 2 * TOK)
    T1 = at("normed", [P, 2, TOK], F32, o_s)
    HF = at("modulated", [P, 2, TOK], F32, o_s + 2 * TOK)
    AROW = at("ada_first_rows", [2, 3, 512], F32, o_h)
    DI0 = at("inv_diag_first", [P, TOK // P, P], F32, o_h + 2048)
    SQ = at("squares", [P, 2, TOK], F32, o_s + 4096)
    SS = at("square_sums", [P, TOK], F32, o_s + 4096 + 2 * TOK)
    WR = at("w_raw", [P, 2, KT, P], F32, o_wr)
    AR = at("ada_raw", [P, 2, 2, 512], F32, o_ar)
    WH = at("w_hi", [P, 4, KT, P], F32R, o_wh)
    WL = at("w_lo", [P, 4, KT, P], F32R, o_wl)
    AC = at("ada_acc", [P, 2, 512], F32, o_acc)
    AT = at("ada_turned", [P, 2, 512], F32, o_acc + 1024)
    DI = at("inv_diag", [P, TOK // P, P], F32, o_acc)
    EE = at("probs", [P, 2, 2, 512], F32, o_acc)
    w = o_misc
    CO = at("consts", [P, NCONST], F32, w)
    w += NCONST
    SELR = at("selector", [P, P], F32R, w)
    w += P
    MSKR = at("window_masks", [P, 3, 32], F32R, w)
    w += 96
    ONES = at("ones", [P, P], F32, w)
    w += P
    PT_ = at("params", [P, 176], F32, w)
    w += 176
    ADA = at("ada", [P, 2, 2, 48], F32, w)
    w += 192
    AM = at("scale_terms", [P, 4, 2, KT], F32, w)
    w += 64
    CSI = at("silu_c", [P, KT, 2], F32, w)
    w += 16
    FOLD = at("fold", [P, P], F32, o_end)
    AQ = at("ada_quarters", [P, 4, 32], F32, o_end + P)
    CT = at("silu_tmp", [P, 3, 16], F32, o_acc + 1024)
    RMS = at("rms", [P, 2, 8], F32, w)
    w += 16
    EPSC = at("epsilon", [P, 1], F32, w)
    w += 8
    SM = at("softmax_small", [P, 2, 5, 2], F32, w)
    assert w <= o_end
    IDN = CO[:, 0:P]

    scratch = nc.dram_tensor("rpb_scratch", (HEADS, BHEAD), F32).ap()

    bias_rows = nc.dram_tensor("bias_rows_dram", (P, HEADS, BRUN), F32).ap()

    with ExitStack() as es:
        PS = es.enter_context(nc.psum_tensor("ps", [P, 4, 1024], F32))
        PSB = PS[:, :, :].rearrange("p s (b n) -> p (s b) n", b=2)

        def sem(name):
            return es.enter_context(nc.semaphore(name))

        x_in = [sem(f"x_in{t}") for t in range(TOK // P)]
        pa_in, pb_in, const_in, fold_in, rpb_in, scratch_in = map(sem, (
            "pa_in", "pb_in", "const_in", "fold_in", "rpb_in", "scratch_in"))
        af_in = [sem(f"ada_first_in{k}") for k in range(KT)]
        w_in = [sem(f"w_in{s}") for s in range(2)]
        a_in = [sem(f"ada_in{s}") for s in range(2)]
        rows_in, out_done = map(sem, ("rows_in", "out_done"))
        bias_in = [sem(f"bias_in{b}") for b in range(2)]
        x_ctx, af_step = map(sem, ("x_ctx", "ada_first_step"))
        ones_set, rpb_zero, rpb_rev, par_t, sel_set, silu_e, silu_d, silu_r, silu_done, af_mm, af_rows = map(sem, (
            "ones_set", "rpb_zero", "rpb_rev", "par_t", "sel_set", "silu_e", "silu_d", "silu_r", "silu_done",
            "ada_first_mm", "ada_first_rows"))
        hi_done, lo_done, units_done, act_evac, dve_evac = map(sem, (
            "hi_done", "lo_done", "units_done", "act_evac", "dve_evac"))
        ada_used, ada_red, ada_step, ada_turned, ada_part, ada_set, am_set = map(sem, (
            "ada_used", "ada_red", "ada_step", "ada_turned", "ada_part", "ada_set", "am_set"))
        sq_done, ss_done, ms_done, rms_done, rec_done, diag_done, inv_done = map(sem, (
            "sq_done", "ss_done", "ms_done", "rms_done", "rec_done", "diag_done", "inv_done"))
        t1_done, hf_lat, hf_ctx, h_hi, h_done = map(sem, ("t1_done", "hf_lat", "hf_ctx", "h_hi", "h_done"))
        y_done, y_mid, g_hi, g_done, a_done = map(sem, ("y_done", "y_mid", "g_hi", "g_done", "a_done"))
        part_mm, part_hi, part_done, out_mm, out_taken = map(sem, (
            "part_mm", "part_hi", "part_done", "out_mm", "out_taken"))
        s_mm, m_ctx, m_all, m_neg, e_done, r_done, p_done, pt_mm, pt_hi, pt_done, o_mm, o_hi, o_done = map(sem, (
            "s_mm", "m_ctx", "m_all", "m_neg", "e_done", "r_done", "p_done", "pt_mm", "pt_hi", "pt_done",
            "o_mm", "o_hi", "o_done"))
        xg_done, turned = map(sem, ("xg_done", "turned"))
        row_done = [sem("row_done_vector"), sem("row_done_scalar")]

        block = es.enter_context(nc.Block())

        def norm_count(n):
            return 2 * min(n, 3) + max(n - 3, 0)

        SEG = {TOK: [(0, LAT), (LAT, TOK)], LAT: [(0, LAT)]}

        def evac_counts(phase, i, s):
            if phase == "conv_in":
                return 2 + i * 4 + (s + 2) // 3, PRO + i * 8 + (s - (s + 2) // 3)
            if phase == "conv_out":
                from_conv_in = (min(s, 0) + 2) // 3
                return 2 + KT + from_conv_in, PRO + 2 * KT + s - from_conv_in
            a, d = {"mlp0": (2 + KT, PRO + 3 * KT), "mlp1": (2 + KT + CHUNKS * KT, PRO + (4 + CHUNKS) * KT),
                    "attn_out": (2 + KT + CHUNKS * KT, PRO + (3 + CHUNKS) * KT)}[phase]
            if phase == "attn_out":
                return a, d + s
            return a + i * KT + min(max(s, 0), KT), d + i * KT + min(s, 0) + max(s - KT, 0)

        def part_count(g, n):
            return PARTS_FIRST + PARTS_GROUP * g + sum(len(PARTS[m]) for m in range(n))

        def parts(g, n):
            return [part for part in PARTS[n] if g < GROUPS - 1 or part[1] == 1 and part[0] != "v"]

        def parts_of_unit(u):
            return (1, 3, 6, 6)[u] if u < 4 else PARTS_FIRST + PARTS_GROUP * ((u - 4) // 6) + UNIT_PARTS[(u - 4) % 6]

        def splits(g, n):
            if g == GROUPS - 1:
                return [U_ATTN_OUT - U_ATTN + u for u in OUT_SPLITS.get(n, ())]
            return [6 + 6 * g + n] if n < 6 else []

        def row_halves(t):
            return [(OUTB[:, t, 0:512], PS[:, t, 512:]), (OUTB[:, t, 512:], PS[:, t, 0:512])]

        def item_pair(g, n):
            return 2 * g + n // 4

        def unit_index(phase, i, s):
            return {"conv_in": U_CONV_IN + i * 12, "conv_out": U_CONV_OUT, "mlp0": U_MLP[0] + i * 16,
                    "attn": U_ATTN + i * 12, "attn_out": U_ATTN_OUT, "mlp1": U_MLP[1] + i * 16}[phase] + s

        ADA_CONV = [[(s // 3, q) for q in ((0, 1), (2,), (3,))[s % 3]] if s < 9 else [] for s in range(12)]
        RED_CONV = {7: 0, 10: 1, 11: 2}
        ADA_OUT = [[(0, 0), (0, 1)], [(0, 2)], [(0, 3), (1, 0)], [(1, 1), (1, 2)], [(1, 3)], [], [], []]
        RED_OUT = {4: 0, 7: 1}
        ADA_MLP = [[(s // 4, s % 4)] if s < 12 else [] for s in range(16)]
        RED_MLP = {8: 0, 10: 1, 14: 2}

        @block.sync
        def _(sp):
            for r, src in ((0, norm1_g.rearrange("l (k p) -> (l k) p", p=P)),
                           (16, norm2_g.rearrange("l (k p) -> (l k) p", p=P)),
                           (32, final_g.rearrange("(k p) -> k p", p=P))):
                sp.dma_start(PRA[r:r + src.shape[0], :], src).then_inc(pa_in, 16)
            sp.dma_start(PRB[:, :], ada_b.rearrange("l (k p) -> (l k) p", p=P)).then_inc(pb_in, 16)
            for t in range(0, TOK // P, 2):
                src = x[0, t * P:(t + 1) * P, :] if t < 4 else ctx[0, (t - 4) * P:(t - 3) * P, :]
                sp.dma_start(XN[:, t, :], src).then_inc(x_in[t], 16)
            for k in range(0, KT, 2):
                sp.dma_start(ADAF[:, k, :], ada_w[0, k * P:(k + 1) * P, 0:2 * D]).then_inc(af_in[k], 16)

            def load(phase, i, s, src, dst=None):
                u = unit_index(phase, i, s)
                sp.wait_ge(lo_done, u + 1)
                sp.dma_start(WR[:, s % 2, :, :] if dst is None else dst, src).then_inc(w_in[s % 2], 16)

            cin = conv_in_w[0].rearrange("(k p) n -> p k n", p=P)
            with sp.Fori(1, 3) as i1:
                i = i1 - 1
                for s in range(12):
                    col = (D, 2 * D, 0)[s % 3]
                    load("conv_in", i, s, cin[:, :, bass.ds(i1 * (4 * P) + (s // 3 - 4) * P + col, P)])
            cout = conv_out_w[0].rearrange("(k p) n -> p k n", p=P)
            for s in range(KT):
                load("conv_out", 0, s, cout[:, :, s * P:(s + 1) * P])

            def mlp(layer, phase):
                w1 = mlp_w1[layer].rearrange("(k p) n -> p k n", p=P)
                w2 = mlp_w2[layer].rearrange("(k p) n -> p k n", p=P)
                with sp.Fori(0, CHUNKS) as i:
                    for s in range(KT):
                        load(phase, i, s, w1[:, :, bass.ds(i * D + s * P, P)])
                    for s in range(KT):
                        load(phase, i, KT + s, w2[:, bass.ds(i * KT, KT), s * P:(s + 1) * P])

            mlp(0, "mlp0")
            qkv = attn_qkv_w[0].rearrange("(k p) n -> p k n", p=P)
            def bias_rows_load(pair):
                if pair >= 2:
                    sp.wait_ge(m_neg, 4 * (pair - 1))
                sp.dma_start(BT[:, pair % 2, :, :], bias_rows[:, 2 * pair:2 * pair + 2, :]).then_inc(bias_in[pair % 2], 16)

            def load_qkv(u, what, tile):
                load("attn", 0, u, qkv[:, :, what * D + tile * P:what * D + (tile + 1) * P])

            load_qkv(0, 0, 0)
            load_qkv(1, 1, 0)
            load_qkv(2, 2, 0)
            load_qkv(3, 2, 1)
            sp.wait_ge(rows_in, 16 * ROWS)
            sp.wait_ge(h_done, 3 * KT)
            bias_rows_load(0)
            bias_rows_load(1)
            for g in range(GROUPS):
                u = 4 + 6 * g
                load_qkv(u, 0, 2 * g + 1)
                load_qkv(u + 1, 1, 2 * g + 1)
                if g < GROUPS - 1:
                    load_qkv(u + 2, 0, 2 * g + 2)
                if g:
                    bias_rows_load(2 * g + 1)
                if g < GROUPS - 1:
                    load_qkv(u + 3, 1, 2 * g + 2)
                    load_qkv(u + 4, 2, 2 * g + 2)
                    bias_rows_load(2 * g + 2)
                    load_qkv(u + 5, 2, 2 * g + 3)
            aout = attn_out_w[0].rearrange("(k p) n -> p k n", p=P)
            for s, ((k0, k1, c0, c1), _) in enumerate(OUT_UNITS):
                load("attn_out", 0, s, aout[:, k0:k1, c0 * P:c1 * P],
                     free(WR[:, s % 2, 0, 0:1], [[(c1 - c0) * P, k1 - k0], [1, (c1 - c0) * P]]))
            mlp(1, "mlp1")
            for n, t in enumerate(OUT_ROWS):
                sp.wait_ge(row_done[n % 2], n // 2 + 1)
                sp.dma_start(out[0, t * P:(t + 1) * P, :], OUTB[:, t, :]).then_inc(out_done, 16)
            sp.wait_ge(out_done, 16 * len(OUT_ROWS))

        @block.gpsimd
        def _(pool):
            pool.memset(ONES[:, :], 1.0).then_inc(ones_set, 1)
            pool.memset(EPSC[:, :], EPS).then_inc(ones_set, 1)
            pool.memset(RPB[:, :], 0.0).then_inc(rpb_zero, 1)
            pool.dma_start(RPN[:, :, :], attn_rpb[0]).then_inc(rpb_in, 16)
            pool.wait_ge(rpb_rev, 1)
            pool.dma_start(scratch, RPB[:, :]).then_inc(scratch_in, 16)
            pool.wait_ge(scratch_in, 16)
            for qr in range(ROWS):
                src = bass.AP(scratch.tensor, qr * BPITCH, [[1, WIN], [BHEAD, HEADS], [1, BRUN]])
                pool.dma_start(bias_rows.rearrange("(c r) h n -> r c h n", r=ROWS)[qr], src).then_inc(rows_in, 16)

            def ada_load(layer, entry, slot, block_, quarter):
                pool.wait_ge(ada_used, entry + 1)
                src = ada_w[layer].rearrange("(q k p) n -> p q k n", p=P, k=2)[:, quarter, :, bass.ds(block_ * 512, 512)]
                pool.dma_start(AR[:, slot, :, :], src).then_inc(a_in[slot], 16)

            with pool.Fori(0, 2) as i:
                n = 0
                for entries in ADA_CONV:
                    for b, q in entries:
                        ada_load(0, i * 12 + n, n % 2, i * 3 + 4 + b, q)
                        n += 1
            for n, (b, q) in enumerate(sum(ADA_OUT, [])):
                ada_load(0, 24 + n, n % 2, 10 + b, q)
            with pool.Fori(0, 4) as i:
                n = 0
                for entries in ADA_MLP:
                    for b, q in entries:
                        ada_load(1, i * 12 + 32 + n, n % 2, i * 3 + b, q)
                        n += 1
            with pool.Fori(0, 4) as i:
                for n in range(8):
                    j = n % 4
                    keys = ROWS * WIDTH[j] + CTX
                    pool.wait_ge(r_done, i * 8 + n + 1)
                    e = EE[:, n % 2, :, 0:keys]
                    pool.tensor_tensor(e, e, free(SM[:, n % 2, 4, 0:1], [[1, 2], [0, keys]]), ALU.mult)\
                        .then_inc(p_done, 1)

        @block.tensor
        def _(pe):
            def unit_mms(slot, wslots, hi, lo, tok, ready=None):
                segs = SEG[tok]
                for k in range(KT):
                    for p_ in range(3):
                        wt, rt = ((WH, hi), (WL, hi), (WH, lo))[p_]
                        if ready and p_ != 1:
                            pe.wait_ge(ready[p_ // 2], ready[2] + k + 1)
                        for sl, ws in zip(slot, wslots):
                            for a, b in segs:
                                mm = pe.matmul(PS[:, sl, a:b], wt[:, ws, k, :], rt[:, k, a:b],
                                               start=(k == 0 and p_ == 0), stop=(k == KT - 1 and p_ == 2))
                            if k == KT - 1 and p_ == 2:
                                mm.then_inc(units_done, 1)

            def wait_unit(phase, i, s):
                u = unit_index(phase, i, s)
                pe.wait_ge(lo_done, u + 3)

            def wait_slot(phase, i, s):
                a, d = evac_counts(phase, i, s - 3)
                pe.wait_ge(act_evac, a)
                pe.wait_ge(dve_evac, d)

            def reduce_ada(block_, buf, slot):
                pe.wait_ge(ada_part, block_ + 2)
                pe.matmul(PS[:, slot, TOK:TOK + 32], FOLD[:, :], AQ[:, buf, :], start=True, stop=True).then_inc(ada_red, 1)

            def norm(n, tok):
                pe.wait_ge(ss_done, 6 * (n + 1))
                for sq in (SS, SQ[:, 1, :]):
                    if sq is not SS:
                        pe.wait_ge(sq_done, KT * (n + 1))
                    for g, (a, b) in enumerate(SEG[tok]):
                        for t in range(a // P, b // P):
                            mm = pe.matmul(PS[:, 2, g * 512 + t:g * 512 + t + 1], sq[:, t * P:(t + 1) * P], ONES[:, 0:1],
                                           start=(sq is SS and t == a // P), stop=(sq is not SS), skip_group_check=True)
                        if sq is not SS:
                            mm.then_inc(ms_done, 1)

            def norm_inverse(n, tok):
                for g, (a, b) in enumerate(SEG[tok]):
                    pe.wait_ge(diag_done, norm_count(n) + g + 1)
                    pe.matmul(PS[:, 3, a:b], ONES[:, :], (DI if n else DI0)[:, a // P:b // P, :], start=True, stop=True)\
                        .then_inc(inv_done, 1)

            pe.wait_ge(const_in, 16)
            pe.wait_ge(pa_in, 96)
            pe.transpose(PS[:, 3, 0:80], PRA[:, :], CO[0:80, 0:80]).then_inc(par_t, 1)
            pe.wait_ge(pb_in, 16)
            pe.transpose(PS[:, 3, 512:512 + 96], PRB[:, :], CO[0:96, 0:96]).then_inc(par_t, 1)
            for k in range(KT):
                if k == 3:
                    pe.wait_ge(act_evac, 2)
                if k >= 4:
                    pe.wait_ge(dve_evac, k - 3)
                    pe.wait_ge(x_ctx, k - 3)
                for t in range(TOK // P):
                    if k == 0:
                        pe.wait_ge(x_in[t], 16)
                    mm = pe.transpose(PS[:, k % 4, t * P:(t + 1) * P], XN[:, t, k * P:(k + 1) * P], IDN)
                mm.then_inc(units_done, 1)
            pe.wait_ge(ones_set, 2)
            pe.wait_ge(silu_done, 1)
            pe.wait_ge(dve_evac, 6)
            pe.wait_ge(x_ctx, 6)
            for k in range(KT):
                pe.wait_ge(af_in[k], 16)
                for n in range(3):
                    mm = pe.matmul(PSB[0:2, n, :], CSI[:, k, :], ADAF[:, k, n * 512:(n + 1) * 512],
                                   start=(k == 0), stop=(k == KT - 1), skip_group_check=True)
                    if k == KT - 1:
                        mm.then_inc(af_mm, 1)
                if k == 3:
                    norm(0, TOK)
                if k == 5:
                    norm_inverse(0, TOK)
            for n in range(12):
                if n % 8 == 0:
                    pe.wait_ge(af_rows, n // 8 + 1)
                mm = pe.transpose(PS[:, 2, 2 * n:2 * n + 2], AROW[:, n // 4, n % 4 * P:(n % 4 + 1) * P], CO[0:2, 0:2])
            mm.then_inc(ada_red, 5)
            pe.wait_ge(fold_in, 16)
            pe.wait_ge(ada_part, 1)
            pe.matmul(PS[:, 2, 512:544], FOLD[:, :], AQ[:, 3, :], start=True, stop=True).then_inc(ada_red, 1)

            with pe.Fori(0, 2) as i:
                for s in range(12):
                    if s == 1:
                        continue
                    if s in RED_CONV:
                        wait_slot("conv_in", i, s)
                        reduce_ada(i * 3 + RED_CONV[s], RED_CONV[s], s % 4)
                    if s == 0:
                        wait_unit("conv_in", i, 1)
                        wait_slot("conv_in", i, 1)
                        unit_mms([0, 1], [0, 1], HH, HL, TOK, (h_hi, h_done, 0))
                    else:
                        wait_unit("conv_in", i, s)
                        wait_slot("conv_in", i, s)
                        unit_mms([s % 4], [s % 4], HH, HL, TOK)
            for s in range(KT):
                wait_unit("conv_out", 0, s)
                wait_slot("conv_out", 0, s)
                if s in RED_OUT:
                    reduce_ada(6 + RED_OUT[s], RED_OUT[s], s % 4)
                unit_mms([s % 4], [s % 4], GH_, GL_, TOK, (g_hi, g_done, 0) if s == 0 else None)
            norm(1, TOK)
            norm_inverse(1, TOK)

            def mlp(layer, phase, tok, norm_no):
                def chunk(i, last):
                    for s in range(2 * KT):
                        if s == 1:
                            continue
                        if layer == 0 and s in RED_MLP:
                            wait_slot(phase, i, s)
                            reduce_ada(i * 3 + 8 + RED_MLP[s], RED_MLP[s], s % 4)
                        if s == 0:
                            wait_unit(phase, i, 1)
                            wait_slot(phase, i, 1)
                            unit_mms([0, 1], [0, 1], HH, HL, tok, (h_hi, h_done, norm_no * KT))
                        else:
                            wait_unit(phase, i, s)
                            wait_slot(phase, i, s)
                            if s < KT:
                                unit_mms([s % 4], [s % 4], HH, HL, tok)
                            elif s == KT:
                                unit_mms([s % 4], [s % 4], GH_, GL_, tok,
                                         (g_hi, g_done, KT + layer * CHUNKS * KT + i * KT))
                            else:
                                unit_mms([s % 4], [s % 4], GH_, GL_, tok)
                        if last and s >= KT + 3 and s < KT + 7:
                            turn(s - KT - 3, range(LAT // P))

                with pe.Fori(0, CHUNKS - layer) as i:
                    chunk(i, False)
                if layer:
                    chunk(CHUNKS - 1, True)

            def turn(k, tiles):
                pe.wait_ge(xg_done, k + 1)
                for t in tiles:
                    at_ = (k + 4) % 8 * P
                    mm = pe.transpose(PS[:, t, at_:at_ + P], XG[:, k, t * P:(t + 1) * P], IDN)
                return mm

            mlp(0, "mlp0", TOK, 1)
            norm(2, TOK)
            norm_inverse(2, TOK)

            def scores(g, n):
                pair, j, item = item_pair(g, n), n % 4, 8 * g + n
                loc = ROWS * WIDTH[j]
                if j == 0:
                    pe.wait_ge(part_done, PARTS_FIRST // 2 if pair == 0 else
                               part_count(g, 2) if pair % 2 else part_count(g - 1, 5))
                if item >= 2:
                    pe.wait_ge(e_done, item - 1)
                for hh in range(2):
                    bank = PSB[:, 2 * (n % 2) + hh, :]
                    rows = slice(64 * hh, 64 * hh + 64)
                    pe.matmul(bank[:, 0:loc], SELR[rows, :],
                              free(MSKR[rows, MASK_OF[j], 0:WIDTH[j]], [[1, WIDTH[j]], [0, ROWS]]),
                              start=True, stop=False, skip_group_check=True)
                    for p_, (qt, kt) in enumerate(((QH, KH), (QH, KL), (QL, KH))):
                        q = qt[rows, pair % 2, P * j:P * (j + 1)]
                        at_ = 0
                        if loc == CTX:
                            a = KEYS[j][0][0]
                            mm = pe.matmul(bank[:, 0:2 * CTX], q, free(kt[rows, pair % 2, a:a + 1], [[LAT - a, 2], [1, CTX]]),
                                           start=False, stop=(p_ == 2), skip_group_check=True)
                            continue
                        for a, b in KEYS[j]:
                            pe.matmul(bank[:, at_:at_ + b - a], q, kt[rows, pair % 2, a:b], start=False, stop=False,
                                      skip_group_check=True)
                            at_ += b - a
                        mm = pe.matmul(bank[:, loc:loc + CTX], q, kt[rows, pair % 2, LAT:TOK],
                                       start=False, stop=(p_ == 2), skip_group_check=True)
                mm.then_inc(s_mm, 1)

            def transposes(g, n):
                j, item = n % 4, 8 * g + n
                pe.wait_ge(p_done, item + 1)
                if item >= 1:
                    pe.wait_ge(pt_done, item)
                for t in range(4):
                    for hh in range(2):
                        first = KEY_TILES[j][t][3] if t < 2 else ROWS * WIDTH[j] + (t - 2) * P
                        mm = pe.transpose(PS[:, 2, (2 * t + hh) * P:(2 * t + hh + 1) * P],
                                          EE[:, n % 2, hh, first:first + P], IDN)
                mm.then_inc(pt_mm, 1)

            def values(g, n):
                j, item = n % 4, 8 * g + n
                pe.wait_ge(pt_done, item + 1)
                if item >= 1:
                    pe.wait_ge(o_done, item)
                tiles = [kt[:3] for kt in KEY_TILES[j]] + [(4, 0, P), (5, 0, P)]
                for t, (vt, r0, r1) in enumerate(tiles):
                    for p_, (a, b) in enumerate(((VH, PTH), (VH, PTL), (VL, PTH))):
                        mm = pe.matmul(PSB[:, 6, 0:2 * P],
                                       a[g % 2][vt // 2][r0:r1, vt % 2, n // 4 * P:(n // 4 + 1) * P], b[r0:r1, t, :],
                                       start=(t == 0 and p_ == 0), stop=(t == 3 and p_ == 2), skip_group_check=True)
                mm.then_inc(o_mm, 1)

            def qk_parts(parts_, ready=None):
                for k in range(KT):
                    for p_ in range(3):
                        wt, rt = ((WH, HH), (WL, HH), (WH, HL))[p_]
                        if ready and p_ != 1:
                            pe.wait_ge(ready[p_ // 2], ready[2] + k + 1)
                        for bank, ws, a, b in parts_:
                            mm = pe.matmul(PSB[:, bank, 0:b - a], wt[:, ws, k, :], rt[:, k, a:b],
                                           start=(k == 0 and p_ == 0), stop=(k == KT - 1 and p_ == 2))
                            if k == KT - 1 and p_ == 2:
                                mm.then_inc(part_mm, 1)

            def out_sums(c, bank, rows):
                for k, unit in rows:
                    k0, k1, c0, c1 = OUT_UNITS[unit][0]
                    tile = (k - k0) * (c1 - c0) + c - c0
                    for p_, (wt, ot) in enumerate(((WH, OH), (WL, OH), (WH, OL))):
                        mm = pe.matmul(PSB[:, bank, :], wt[:, unit % 4, tile, :], ot[:, k, :],
                                       start=(k == rows[0][0] and p_ == 0), stop=(k == rows[-1][0] and p_ == 2))
                mm.then_inc(out_mm, 1)

            def out_ahead(c):
                wait_unit("attn_out", 0, max(OUT_OF[c]))
                pe.wait_ge(part_done, PARTS_ALL - 2 if c == 0 else PARTS_ALL)
                if c:
                    pe.wait_ge(out_taken, c)
                out_sums(c, 7, [(k, OUT_OF[c][k // 4]) for k in range(6)])

            def v_part(bank, ws, third):
                for t in range(2):
                    tt = 2 * third + t
                    for k in range(KT):
                        for p_, (ht, wt) in enumerate(((HH, WH), (HL, WH), (HH, WL))):
                            mm = pe.matmul(PSB[:, bank, t * 2 * P:(t + 1) * 2 * P], ht[:, k, tt * P:(tt + 1) * P],
                                           wt[:, ws:ws + 2, k, :], start=(k == 0 and p_ == 0),
                                           stop=(k == KT - 1 and p_ == 2), skip_group_check=True)
                mm.then_inc(part_mm, 1)

            def part(g, what, which, count):
                u = 4 + 6 * g + {"q": 2 * which - 2, "k_lat": 2 * which - 1, "k_ctx": 2 * which - 1, "v": 4}[what]
                wait_unit("attn", 0, u + (what == "v"))
                pe.wait_ge(part_done, count)
                if g == GROUPS - 1 and what != "q":
                    pe.wait_ge(out_taken, 1)
                if what == "v":
                    v_part(7, u % 4, which)
                else:
                    a, b = {"q": (0, LAT), "k_lat": (0, LAT), "k_ctx": (LAT, TOK)}[what]
                    qk_parts([(7, u % 4, a, b)])

            pe.wait_ge(sel_set, 2)
            pe.wait_ge(dve_evac, PRO + (3 + CHUNKS) * KT)
            wait_unit("attn", 0, 1)
            qk_parts([(0, 0, 0, LAT), (2, 1, 0, LAT), (3, 1, LAT, TOK)], (h_hi, h_done, 2 * KT))
            wait_unit("attn", 0, 3)
            v_part(4, 2, 0)
            scores(0, 0)
            v_part(5, 2, 1)
            scores(0, 1)
            v_part(6, 2, 2)
            for g in range(GROUPS):
                for n in range(8):
                    ahead = parts(g, n)
                    if n == 0:
                        pe.wait_ge(part_done, part_count(g, 0))
                    transposes(g, n)
                    if ahead:
                        part(g, *ahead[0], part_count(g, n))
                    if g == GROUPS - 1:
                        for c in OUT_TILES[n][0]:
                            out_ahead(c)
                    values(g, n)
                    if 8 * g + n + 2 < 8 * GROUPS:
                        scores(*divmod(8 * g + n + 2, 8))
                    if len(ahead) > 1:
                        part(g, *ahead[1], part_count(g, n) + 1)
                    if g == GROUPS - 1:
                        for c in OUT_TILES[n][1]:
                            out_ahead(c)
            pe.wait_ge(e_done, 8 * GROUPS)
            pe.wait_ge(o_done, 8 * GROUPS)
            for c in range(KT):
                wait_unit("attn_out", 0, 6 + c // 4)
                if c >= 4:
                    pe.wait_ge(dve_evac, evac_counts("attn_out", 0, c - 3)[1])
                out_sums(c, 2 * (c % 4), [(6, 6 + c // 4), (7, 6 + c // 4)])
            pe.wait_ge(out_mm, 2 * KT)
            pe.nop().then_inc(units_done, U_MLP[1] - U_ATTN)
            norm(3, LAT)
            norm_inverse(3, LAT)
            mlp(1, "mlp1", LAT, 3)
            pe.wait_ge(dve_evac, evac_counts("mlp1", CHUNKS - 1, 15)[1])
            for k in (4, 5, 6):
                turn(k, (0, 1))
            norm(4, LAT)
            for t in (0, 1):
                turn(7, (t,)).then_inc(turned, 1)
            pe.wait_ge(dve_evac, evac_counts("mlp1", CHUNKS - 1, 16)[1])
            for t in (3, 2):
                if t == 2:
                    pe.wait_ge(rms_done, norm_count(5))
                for k in (4, 5, 6, 7):
                    mm = turn(k, (t,))
                mm.then_inc(turned, 1)

        @block.scalar
        def _(act):
            for r, src in ((40, conv_w[0].rearrange("j (k p) -> (j k) p", p=P)),
                           (64, c.rearrange("b (k p) -> (b k) p", p=P)), (72, c_ctx.rearrange("(k p) -> k p", p=P))):
                act.dma_start(PRA[r:r + src.shape[0], :], src).then_inc(pa_in, 16)
            act.dma_start(CO[:, :], consts[:, 0:NCONST]).then_inc(const_in, 16)
            for t in range(1, TOK // P, 2):
                src = x[0, t * P:(t + 1) * P, :] if t < 4 else ctx[0, (t - 4) * P:(t - 3) * P, :]
                act.dma_start(XN[:, t, :], src).then_inc(x_in[t], 16)
            for k in range(1, KT, 2):
                act.dma_start(ADAF[:, k, :], ada_w[0, k * P:(k + 1) * P, 0:2 * D]).then_inc(af_in[k], 16)
            act.dma_start(FOLD[:, :], consts[:, NCONST:NCONST + P]).then_inc(fold_in, 16)

            def split_hi(u, slot, used=None):
                act.wait_ge(w_in[slot % 2], 16 * u[1] + 16)
                if used:
                    act.wait_ge(*used)
                else:
                    act.wait_ge(units_done, u[0] + PRO - 3)
                act.activation(WH[:, slot, :, :], WR[:, slot % 2, :, :], ACT.Copy).then_inc(hi_done, 1)

            def split_ahead(phase, i, s):
                u = unit_index(phase, i, s + 2)
                half = {"conv_in": i * 6, "conv_out": U_CONV_OUT // 2, "mlp0": U_MLP[0] // 2 + i * 8,
                        "attn": U_ATTN // 2 + i * 6, "attn_out": U_ATTN_OUT // 2,
                        "mlp1": U_MLP[1] // 2 + i * 8}[phase] + (s + 2) // 2
                split_hi((u, half), (s + 2) % 4)

            def squares(n, k, wait, tok):
                act.wait_ge(*wait)
                if k >= 3:
                    act.wait_ge(ss_done, 6 * n + k - 2)
                dst = SS if k == 0 else SQ[:, k % 2, :]
                ins = act.activation(dst[:, 0:LAT], XL[:, k, :], ACT.Square)
                if tok > LAT:
                    ins = act.activation(dst[:, LAT:TOK], XC[:, k, :], ACT.Square)
                ins.then_inc(sq_done, 1)

            def root(n, tok):
                for g, (a, b) in enumerate(SEG[tok]):
                    act.wait_ge(ms_done, norm_count(n) + g + 1)
                    act.activation(RMS[:, 0, a // P:b // P], PS[:, 2, g * 512 + a // P:g * 512 + b // P], ACT.Sqrt,
                                   bias=EPSC[:, 0:1], scale=1.0 / D).then_inc(rms_done, 1)

            def norm(n, tok, ada):
                act.wait_ge(am_set, 2 * (n + 1))
                for k in range(KT):
                    act.wait_ge(t1_done, n * KT + k + 1)
                    layer, sh = ada
                    if k >= 2:
                        act.wait_ge(h_done, n * KT + k - 1)
                    for cond, (a, b) in enumerate(SEG[tok]):
                        ins = act.activation(HH[:, k, a:b], T1[:, k % 2, a:b], ACT.Identity,
                                             bias=ADA[:, layer, cond, sh + k:sh + k + 1], scale=AM[:, n, cond, k:k + 1])
                    ins.then_inc(h_hi, 1)
                    act.activation(HF[:, k % 2, 0:LAT], T1[:, k % 2, 0:LAT], ACT.Identity,
                                   bias=ADA[:, layer, 0, sh + k:sh + k + 1], scale=AM[:, n, 0, k:k + 1]).then_inc(hf_lat, 1)

            act.wait_ge(ones_set, 2)
            act.wait_ge(par_t, 1)
            act.activation(PT_[:, 0:80], PS[:, 3, 0:80], ACT.Copy).then_inc(act_evac, 1)
            act.wait_ge(par_t, 2)
            act.activation(PT_[:, 80:176], PS[:, 3, 512:608], ACT.Copy).then_inc(act_evac, 1)
            act.wait_ge(act_evac, 2)
            act.activation(CT[:, 0, :], PT_[:, 64:80], ACT.Exp, scale=-1.0).then_inc(silu_e, 1)
            act.wait_ge(const_in, 16)
            act.activation(SELR[:, :], CO[:, P:2 * P], ACT.Copy).then_inc(sel_set, 1)
            act.activation(MSKR[:, :, :], CO[:, 2 * P:].rearrange("p (m c) -> p m c", m=3), ACT.Copy).then_inc(sel_set, 1)
            for k in range(KT):
                act.wait_ge(units_done, k + 1)
                act.activation(XC[:, k, :], PS[:, k % 4, LAT:TOK], ACT.Copy).then_inc(x_ctx, 1)
                act.wait_ge(x_ctx, k + 1)
                squares(0, k, (dve_evac, k + 1), TOK)
            root(0, TOK)
            split_hi((0, 0), 0)
            split_hi((1, 0), 1)
            for a, b in ((0, 2), (2, 3)):
                act.wait_ge(af_mm, b)
                act.activation(AROW[:, a:b, :], PSB[0:2, a:b, :], ACT.Copy).then_inc(af_rows, 1)
            norm(0, TOK, (0, 0))

            with act.Fori(0, 2) as i:
                for s in range(12):
                    split_ahead("conv_in", i, s)
                    t = s // 3
                    if s % 3 == 0:
                        act.wait_ge(units_done, PRO + 12 * i + s + 1)
                        act.activation(CS_[:, t % 2, :], PS[:, s % 4, 0:TOK], ACT.Copy).then_inc(act_evac, 1)
                    elif s % 3 == 1:
                        act.wait_ge(dve_evac, PRO + 8 * i + 2 * t + 1)
                        act.activation(YY[:, t % 2, 0:TOK + 1], UU[:, t % 2, 0:TOK + 1], ACT.Copy,
                                       scale=PT_[:, bass.ds(i * 4 + 40 + t, 1)]).then_inc(y_done, 1)
                    else:
                        act.wait_ge(dve_evac, PRO + 8 * i + 2 * t + 2)
                        act.activation(GH_[:, bass.ds(i * 4 + t, 1), :].rearrange("p a n -> p (a n)"),
                                       GF[:, t % 2, :], ACT.Copy).then_inc(g_hi, 1)
            for s in range(KT):
                split_ahead("conv_out", 0, s)
                squares(1, s, (dve_evac, PRO + 2 * KT + s + 1), TOK)
            root(1, TOK)
            norm(1, TOK, (0, 24))

            def mlp(layer, phase, tok, norm_next):
                tiles = KT + layer * CHUNKS * KT

                def chunk(i, last):
                    for s in range(2 * KT):
                        if not (last and layer == 1 and s >= 2 * KT - 2):
                            split_ahead(phase, i, s)
                        if s < KT:
                            act.wait_ge(units_done, unit_index(phase, i, s) + PRO + 1)
                            act.wait_ge(a_done, i * KT + layer * CHUNKS * KT + s + 1)
                            act.activation(RR[:, s % 2, 0:tok], PS[:, s % 4, 0:tok], ACT.Relu).then_inc(act_evac, 1)
                            act.wait_ge(act_evac, evac_counts(phase, i, s + 1)[0])
                            act.activation(GH_[:, s, 0:tok], RR[:, s % 2, 0:tok], ACT.Square).then_inc(g_hi, 1)
                        elif last:
                            squares(norm_next, s - KT, (dve_evac, evac_counts(phase, i, s + 1)[1]), tok)
                            if layer:
                                act.activation(XG[:, s - KT, :], XL[:, s - KT, :], ACT.Copy,
                                               scale=PT_[:, 32 + s - KT:33 + s - KT]).then_inc(xg_done, 1)

                with act.Fori(0, CHUNKS - 1) as i:
                    chunk(i, False)
                chunk(CHUNKS - 1, True)

            def split_attn(u):
                used = None
                if u >= 4:
                    used = (part_mm, parts_of_unit(u - 4)) if u < 28 else (out_mm, OUT_UNITS[u - 28][1])
                split_hi((U_ATTN + u, (U_ATTN + u) // 2), u % 4, used)

            mlp(0, "mlp0", TOK, 2)
            root(2, TOK)
            split_attn(2)
            norm(2, TOK, (1, 0))
            split_attn(3)

            def exps(g, n):
                keys = ROWS * WIDTH[n % 4] + CTX
                act.wait_ge(m_neg, 8 * g + n + 1)
                for hh in range(2):
                    ins = act.activation(EE[:, n % 2, hh, 0:keys], PSB[:, 2 * (n % 2) + hh, 0:keys], ACT.Exp,
                                         bias=SM[:, n % 2, 2, hh:hh + 1], accum_out=SM[:, n % 2, 3, hh:hh + 1])
                ins.then_inc(e_done, 1)

            def take_hi(what, which, g, count, bank):
                act.wait_ge(part_mm, count)
                if what == "v":
                    if g >= 2:
                        act.wait_ge(o_mm, 8 * (g - 1))
                    act.activation(VH[g % 2][which][:, :, :], PSB[:, bank, :].rearrange("p (t n) -> p t n", t=2),
                                   ACT.Copy).then_inc(part_hi, 1)
                    return
                if which >= 2:
                    act.wait_ge(s_mm, 4 * (which - 1))
                if what == "q":
                    for a, b, to in Q_ORDER:
                        ins = act.activation(QH[:, which % 2, to:to + b - a], PSB[:, bank, a:b], ACT.Copy, scale=ATTN_SCALE)
                    ins.then_inc(part_hi, 1)
                else:
                    a, b = (0, LAT) if what == "k_lat" else (LAT, TOK)
                    act.activation(KH[:, which % 2, a:b], PSB[:, bank, 0:b - a], ACT.Copy).then_inc(part_hi, 1)

            take_hi("q", 0, 0, 1, 0)
            take_hi("k_lat", 0, 0, 2, 2)
            take_hi("k_ctx", 0, 0, 3, 3)
            split_attn(4)
            take_hi("v", 0, 0, 4, 4)
            exps(0, 0)
            split_attn(5)
            take_hi("v", 1, 0, 5, 5)
            take_hi("v", 2, 0, 6, 6)
            for g in range(GROUPS):
                for n in range(8):
                    item = 8 * g + n
                    act.wait_ge(pt_mm, item + 1)
                    act.activation(PTH[:, :, :].rearrange("p t n -> p (t n)"), PS[:, 2, :], ACT.Copy).then_inc(pt_hi, 1)
                    if item + 1 < 8 * GROUPS:
                        exps(*divmod(item + 1, 8))
                    ahead = parts(g, n)
                    for u in splits(g, n):
                        split_attn(u)
                    if ahead:
                        what, which = ahead[0]
                        take_hi(what, which + (0 if what == "v" else 2 * g), g + 1, part_count(g, n) + 1, 7)
                    act.wait_ge(o_mm, item + 1)
                    for hh in range(2):
                        rows = slice(64 * hh, 64 * hh + 64)
                        ins = act.activation(OH[rows, item_pair(g, n), P * (n % 4):P * (n % 4 + 1)],
                                             PSB[rows, 6, hh * P:(hh + 1) * P], ACT.Copy)
                    ins.then_inc(o_hi, 1)
                    if len(ahead) > 1:
                        take_hi(ahead[1][0], ahead[1][1] + 2 * g, g + 1, part_count(g, n) + 2, 7)
            act.activation(RMS[:, 0, 7:8], EPSC[:, 0:1], ACT.Sqrt)
            split_attn(U_MLP[1] - U_ATTN)
            for s in range(KT):
                squares(3, s, (dve_evac, PRO + (3 + CHUNKS) * KT + s + 1), LAT)
            root(3, LAT)
            split_attn(U_MLP[1] - U_ATTN + 1)
            norm(3, LAT, (1, 24))
            mlp(1, "mlp1", LAT, 4)
            root(4, LAT)
            act.wait_ge(rec_done, norm_count(5))
            for n in (1, 3):
                t = OUT_ROWS[n]
                act.wait_ge(turned, n + 1)
                for to, src in row_halves(t):
                    ins = act.activation(to, src, ACT.Copy, scale=RMS[:, 1, t:t + 1])
                ins.then_inc(row_done[1], 1)

        @block.vector
        def _(dve):
            def split_lo(u, slot):
                dve.wait_ge(hi_done, u + 1)
                dve.tensor_tensor(WL[:, slot, :, :], WR[:, slot % 2, :, :], WH[:, slot, :, :].bitcast(F32),
                                  ALU.subtract).then_inc(lo_done, 1)

            def split_attn(u):
                split_lo(U_ATTN + u, u % 4)

            def split_ahead(phase, i, s):
                split_lo(unit_index(phase, i, s + 2), (s + 2) % 4)

            def sums(n, k, tok):
                if k == 0 or k == KT - 1:
                    return
                dve.wait_ge(sq_done, n * KT + k + 1)
                if k >= 2:
                    dve.wait_ge(ss_done, 6 * n + k - 1)
                dve.tensor_tensor(SS[:, 0:tok], SS[:, 0:tok], SQ[:, k % 2, 0:tok], ALU.add).then_inc(ss_done, 1)

            def inverse_rms(n, g, t0, t1_):
                dve.wait_ge(rms_done, norm_count(n) + g + 1)
                dve.reciprocal(RMS[:, 1, t0:t1_], RMS[:, 0, t0:t1_]).then_inc(rec_done, 1)

            def norm(n, tok, ada, meanwhile=None):
                for g, (a, b) in enumerate(SEG[tok]):
                    t0, t1_ = a // P, b // P
                    inverse_rms(n, g, t0, t1_)
                    dve.wait_ge(rec_done, norm_count(n) + g + 1)
                    dve.tensor_tensor((DI if n else DI0)[:, t0:t1_, :], free(IDN, [[0, t1_ - t0], [1, P]]),
                                      free(RMS[:, 1, t0:t1_], [[1, t1_ - t0], [0, P]]), ALU.mult).then_inc(diag_done, 1)
                if meanwhile:
                    meanwhile()

                def t1(k):
                    if k >= 2:
                        dve.wait_ge(hf_lat, n * KT + k - 1)
                    if k == 0:
                        dve.wait_ge(inv_done, norm_count(n) + 1)
                    if n == 2:
                        for a, dims in ((0, [[COLS - 8, 2], [1, 8], [COLS, ROWS]]), (8, [[1, COLS - 16], [COLS, ROWS]])):
                            ins = dve.tensor_tensor(T1[:, k % 2, a * WIN:a * WIN + ROWS * (16 if a == 0 else COLS - 16)],
                                                    free(XL[:, k, a:a + 1], dims), free(PS[:, 3, a:a + 1], dims), ALU.mult)
                    else:
                        ins = dve.tensor_tensor(T1[:, k % 2, 0:LAT], XL[:, k, :], PS[:, 3, 0:LAT], ALU.mult)
                    if tok > LAT:
                        if k == 0:
                            dve.wait_ge(inv_done, norm_count(n) + 2)
                        ins = dve.tensor_tensor(T1[:, k % 2, LAT:TOK], XC[:, k, :], PS[:, 3, LAT:TOK], ALU.mult)
                    ins.then_inc(t1_done, 1)

                t1(0)
                for k in range(KT):
                    layer, sh = ada
                    if tok > LAT:
                        dve.wait_ge(t1_done, n * KT + k + 1)
                        dve.tensor_scalar(HF[:, k % 2, LAT:TOK], T1[:, k % 2, LAT:TOK], AM[:, n, 1, k:k + 1],
                                          ADA[:, layer, 1, sh + k:sh + k + 1], ALU.mult, ALU.add).then_inc(hf_ctx, 1)
                    if k + 1 < KT:
                        t1(k + 1)
                    if tok > LAT:
                        dve.wait_ge(hf_ctx, n * KT + k + 1)
                    dve.wait_ge(h_hi, n * KT + k + 1)
                    dve.wait_ge(hf_lat, n * KT + k + 1)
                    dve.tensor_tensor(HL[:, k, 0:tok], HF[:, k % 2, 0:tok], HH[:, k, 0:tok].bitcast(F32),
                                      ALU.subtract).then_inc(h_done, 1)

            def scale_terms(n, layer, gcol, sc, count):
                dve.wait_ge(ada_set, count)
                for cond in range(2):
                    dve.scalar_tensor_tensor(AM[:, n, cond, :], ADA[:, layer, cond, sc:sc + KT], 1.0,
                                             PT_[:, gcol:gcol + KT], ALU.add, ALU.mult).then_inc(am_set, 1)

            def turn_sums(before, b, reduced=None):
                dve.transpose(AT[:, :, :].rearrange("p c n -> p (c n)"), AC[:, :, :].rearrange("p c n -> p (c n)"))\
                    .then_inc(ada_turned, 1)
                dve.wait_ge(ada_turned, before + 1)
                if reduced is not None:
                    dve.wait_ge(ada_red, reduced)
                dve.reduce_sum(AQ[:, b, :], AT[:, :, :].rearrange("p c (j n) -> p (c j) n", n=32), AX_X)\
                    .then_inc(ada_part, 1)

            def ada_entry(layer, block_, b, q, half, slot):
                entry = block_ * 4 + q
                dve.wait_ge(a_in[slot], 16 * half + 16)
                for kk in range(2):
                    for cond in range(2):
                        sc = CSI[:, 2 * q + kk, cond:cond + 1]
                        a = AC[:, cond, :]
                        first = q == 0 and kk == 0
                        if kk:
                            dve.wait_ge(ada_step, entry * 3 + cond + 1)
                        elif not first:
                            dve.wait_ge(*((ada_used, entry + 2) if cond else (ada_step, entry * 3)))
                        if first:
                            ins = dve.tensor_scalar(a, AR[:, slot, kk, :], sc, None, ALU.mult)
                        else:
                            ins = dve.scalar_tensor_tensor(a, AR[:, slot, kk, :], sc, a, ALU.mult, ALU.add)
                        ins.then_inc(ada_used if kk and cond else ada_step, 1)
                if q == 3:
                    dve.wait_ge(ada_step, entry * 3 + 3)
                    dve.wait_ge(ada_used, entry + 3)
                    turn_sums(block_ + 1, b, block_ + 4)

            def ada_out(layer, at_, tile):
                for a in range(4):
                    rows = slice(32 * a, 32 * a + 32)
                    dve.tensor_tensor(ADA[rows, layer, :, bass.ds(tile, 4)],
                                      free(PS[rows, at_[0], at_[1] + a:at_[1] + a + 1], [[16, 2], [4, 4]]),
                                      PT_[rows, bass.ds(tile + 80 + 48 * layer, 4)].rearrange("p (c t) -> p c t", c=1)
                                      .to_broadcast([32, 2, 4]), ALU.add).then_inc(ada_set, 1)

            def residual(slot, k, layer, gate, tok, by_column=False):
                y, xk = PS[:, 3, 512:1024] if slot is None else PS[:, slot, 0:LAT], XL[:, k, :]
                if by_column:
                    y = y.rearrange("p (c r) -> p r c", r=ROWS)
                    xk = xk.rearrange("p (r c) -> p r c", r=ROWS)
                ins = dve.scalar_tensor_tensor(xk, y, ADA[:, layer, 0, gate + k:gate + k + 1], xk, ALU.mult, ALU.add)
                if tok > LAT:
                    ins = dve.scalar_tensor_tensor(XC[:, k, :], PS[:, slot, LAT:TOK],
                                                   ADA[:, layer, 1, gate + k:gate + k + 1], XC[:, k, :], ALU.mult, ALU.add)
                ins.then_inc(out_taken if slot is None else dve_evac, 1)

            for what in (lo_done, lo_done, ada_used, ada_used, a_done, a_done):
                dve.engine_nop().then_inc(what, 1)
            for k in range(KT):
                dve.wait_ge(units_done, k + 1)
                dve.tensor_copy(XL[:, k, :], PS[:, k % 4, 0:LAT]).then_inc(dve_evac, 1)
                if k == 1:
                    dve.wait_ge(silu_e, 1)
                    dve.tensor_scalar(CT[:, 1, :], CT[:, 0, :], 1.0, None, ALU.add).then_inc(silu_d, 1)
                    dve.wait_ge(silu_d, 1)
                    dve.reciprocal(CT[:, 2, :], CT[:, 1, :]).then_inc(silu_r, 1)
                    dve.wait_ge(silu_r, 1)
                    dve.tensor_tensor(CSI[:, :, :], PT_[:, 64:80].rearrange("p (a k) -> p k a", a=2),
                                      CT[:, 2, :].rearrange("p (a k) -> p k a", a=2), ALU.mult).then_inc(silu_done, 1)
                if k == 3:
                    dve.wait_ge(rpb_zero, 1)
                    dve.wait_ge(rpb_in, 16)
                    dve.tensor_copy(free(RPB[:, 711:712], [[-BPITCH, 15], [-1, 31]]), RPN[:, :, :]).then_inc(rpb_rev, 1)
                if k >= 1:
                    sums(0, k - 1, TOK)

            def ada_first_block(k):
                dve.wait_ge(af_in[k], 16)
                for cond in range(2):
                    a, w_, sc = AC[:, cond, :], ADAF[:, k, 3 * 512:4 * 512], CSI[:, k, cond:cond + 1]
                    if k:
                        dve.wait_ge(af_step, 2 * k - 1 + cond)
                        ins = dve.scalar_tensor_tensor(a, w_, sc, a, ALU.mult, ALU.add)
                    else:
                        dve.wait_ge(silu_done, 1)
                        ins = dve.tensor_scalar(a, w_, sc, None, ALU.mult)
                    ins.then_inc(af_step, 1)

            for k in range(3):
                ada_first_block(k)

            def first_ada():
                for k in range(3, KT):
                    if k >= 6:
                        split_lo(k - 6, k - 6)
                    ada_first_block(k)
                dve.wait_ge(af_step, 2 * KT)
                turn_sums(0, 3)
                dve.wait_ge(scratch_in, 16)
                dve.wait_ge(ada_red, 6)
                for cond in range(2):
                    dve.tensor_tensor(ADA[:, 0, cond, 0:12], free(PS[:, 2, cond:cond + 1], [[2, 12]]), PT_[:, 80:92],
                                      ALU.add).then_inc(ada_set, 1)
                ada_out(0, (2, 512), 12)
                scale_terms(0, 0, 0, 8, 6)

            norm(0, TOK, (0, 0), first_ada)

            dve.wait_ge(h_done, KT)
            for col in (0, LAT + 1, TOK + 2):
                dve.memset(UU[:, :, col:col + 1], 0.0)
            with dve.Fori(0, 2) as i:
                n = 0
                for s in range(12):
                    split_ahead("conv_in", i, s)
                    t = s // 3
                    y = YY[:, t % 2, 0:TOK + 1]
                    if s % 3 == 2:
                        dve.wait_ge(y_done, 4 * i + t + 1)
                        for tap in (1, 2):
                            dve.scalar_tensor_tensor(y, UU[:, t % 2, tap:tap + TOK + 1],
                                                     PT_[:, bass.ds(i * 4 + 40 + KT * tap + t, 1)], y,
                                                     ALU.mult, ALU.add).then_inc(y_mid, 1)
                            dve.wait_ge(y_mid, 8 * i + 2 * t + tap)
                    if s % 3:
                        dve.wait_ge(units_done, PRO + 12 * i + s + 1)
                        if s in RED_CONV:
                            ada_out(0, (s % 4, TOK), (i * 3 + 4 + RED_CONV[s]) * 4)
                    if s % 3 == 1:
                        if t:
                            dve.wait_ge(g_done, 4 * i + t)
                        dve.wait_ge(act_evac, evac_counts("conv_in", i, s)[0])
                        dve.tensor_tensor(UU[:, t % 2, 1:LAT + 1], PS[:, s % 4, 0:LAT], CS_[:, t % 2, 0:LAT], ALU.mult)
                        dve.tensor_tensor(UU[:, t % 2, LAT + 2:TOK + 2], PS[:, s % 4, LAT:TOK], CS_[:, t % 2, LAT:TOK],
                                          ALU.mult).then_inc(dve_evac, 1)
                    elif s % 3 == 2:
                        dve.tensor_tensor(GF[:, t % 2, 0:LAT], PS[:, s % 4, 0:LAT], YY[:, t % 2, 0:LAT], ALU.mult)
                        dve.tensor_tensor(GF[:, t % 2, LAT:TOK], PS[:, s % 4, LAT:TOK], YY[:, t % 2, LAT + 1:TOK + 1],
                                          ALU.mult).then_inc(dve_evac, 1)
                        dve.wait_ge(g_hi, 4 * i + t + 1)
                        hi = GH_[:, bass.ds(i * 4 + t, 1), :].bitcast(F32).rearrange("p a n -> p (a n)")
                        dve.tensor_tensor(GL_[:, bass.ds(i * 4 + t, 1), :].rearrange("p a n -> p (a n)"),
                                          GF[:, t % 2, :], hi, ALU.subtract).then_inc(g_done, 1)
                    for b, q in ADA_CONV[s]:
                        ada_entry(0, i * 3 + b, b, q, i * 6 + n // 2, n % 2)
                        n += 1
            scale_terms(1, 0, 16, 32, 30)
            n = 0
            for s in range(KT):
                split_ahead("conv_out", 0, s)
                for b, q in ADA_OUT[s]:
                    ada_entry(0, 6 + b, b, q, 12 + n // 2, n % 2)
                    n += 1
                dve.wait_ge(units_done, PRO + U_CONV_OUT + s + 1)
                if s in RED_OUT:
                    ada_out(0, (s % 4, TOK), (10 + RED_OUT[s]) * 4)
                residual(s % 4, s, 0, 16, TOK)
                if s:
                    sums(1, s - 1, TOK)
            sums(1, KT - 1, TOK)
            dve.wait_ge(ada_set, 38)
            norm(1, TOK, (0, 24))

            def mlp(layer, phase, tok, norm_next):
                tiles = layer * CHUNKS * KT

                def chunk(i, last):
                    n = 0
                    for s in range(2 * KT):
                        if not (last and layer == 1 and s >= 2 * KT - 2):
                            split_ahead(phase, i, s)
                        if layer == 0:
                            for b, q in ADA_MLP[s]:
                                ada_entry(1, i * 3 + 8 + b, b, q, i * 6 + 16 + n // 2, n % 2)
                                n += 1
                        if s < KT:
                            dve.wait_ge(act_evac, evac_counts(phase, i, s + 1)[0])
                            dve.wait_ge(g_done, i * KT + KT + tiles + s - 1)
                            r = RR[:, s % 2, 0:tok]
                            dve.tensor_tensor(AA[:, s % 2, 0:tok], r, r, ALU.mult).then_inc(a_done, 1)
                            dve.wait_ge(a_done, i * KT + 2 + tiles + s + 1)
                            dve.wait_ge(g_hi, i * KT + KT + tiles + s + 1)
                            dve.tensor_tensor(GL_[:, s, 0:tok], AA[:, s % 2, 0:tok], GH_[:, s, 0:tok].bitcast(F32),
                                              ALU.subtract).then_inc(g_done, 1)
                        else:
                            dve.wait_ge(units_done, unit_index(phase, i, s) + PRO + 1)
                            if layer == 0 and s in RED_MLP:
                                ada_out(1, (s % 4, TOK), (i * 3 + RED_MLP[s]) * 4)
                            residual(s % 4, s - KT, layer, 40, tok)
                            if last and s > KT:
                                sums(norm_next, s - KT - 1, tok)

                with dve.Fori(0, CHUNKS - 1) as i:
                    chunk(i, False)
                chunk(CHUNKS - 1, True)
                sums(norm_next, KT - 1, tok)

            mlp(0, "mlp0", TOK, 2)
            scale_terms(2, 1, KT, 8, 86)
            scale_terms(3, 1, 3 * KT, 32, 86)
            norm(2, TOK, (1, 0), lambda: split_attn(2))
            split_attn(3)

            def maxima(g, n):
                wide, pair, item = WIDTH[n % 4], item_pair(g, n), 8 * g + n
                loc = ROWS * wide
                b0 = 2 * (n % 2)
                if n % 4 == 0:
                    dve.wait_ge(bias_in[pair % 2], 16 * (pair // 2 + 1))
                dve.wait_ge(s_mm, item + 1)
                dve.reduce_max(SM[:, n % 2, 0, :], PSB[:, b0:b0 + 2, loc:loc + CTX], AX_X,
                               negate=True).then_inc(m_ctx, 1)
                for hh in range(2):
                    s_loc = PSB[:, b0 + hh, 0:loc].rearrange("p (c r) -> p c r", r=ROWS)
                    last = BRUN - 1 - (8 if n % 4 == 0 else 0)
                    bias = free(BT[:, pair % 2, hh, last:last + 1], [[-1, wide], [-BPITCH, ROWS]])
                    dve.tensor_tensor_reduce(s_loc, s_loc, bias, 1.0, LOWEST, ALU.add,
                                             ALU.max, SM[:, n % 2, 1, hh:hh + 1]).then_inc(m_all, 1)
                dve.wait_ge(m_all, 2 * item + 2)
                dve.wait_ge(m_ctx, item + 1)
                dve.scalar_tensor_tensor(SM[:, n % 2, 2, :], SM[:, n % 2, 1, :], -1.0, SM[:, n % 2, 0, :],
                                         ALU.mult, ALU.min).then_inc(m_neg, 1)

            def recip(g, n):
                dve.wait_ge(e_done, 8 * g + n + 1)
                dve.reciprocal(SM[:, n % 2, 4, :], SM[:, n % 2, 3, :]).then_inc(r_done, 1)

            def take_lo(what, which, g, count, bank):
                dve.wait_ge(part_hi, count)
                if what == "v":
                    dve.tensor_tensor(VL[g % 2][which][:, :, :], PSB[:, bank, :].rearrange("p (t n) -> p t n", t=2),
                                      VH[g % 2][which][:, :, :].bitcast(F32), ALU.subtract).then_inc(part_done, 1)
                elif what == "q":
                    for a, b, to in Q_ORDER:
                        ins = dve.scalar_tensor_tensor(
                            QL[:, which % 2, to:to + b - a], PSB[:, bank, a:b], ATTN_SCALE,
                            QH[:, which % 2, to:to + b - a].bitcast(F32), ALU.mult, ALU.subtract)
                    ins.then_inc(part_done, 1)
                else:
                    a, b = (0, LAT) if what == "k_lat" else (LAT, TOK)
                    dve.tensor_tensor(KL[:, which % 2, a:b], PSB[:, bank, 0:b - a], KH[:, which % 2, a:b].bitcast(F32),
                                      ALU.subtract).then_inc(part_done, 1)

            def out_residual(c):
                dve.wait_ge(out_mm, c + 1)
                residual(None, c, 1, 16, LAT, by_column=True)

            take_lo("q", 0, 0, 1, 0)
            take_lo("k_lat", 0, 0, 2, 2)
            take_lo("k_ctx", 0, 0, 3, 3)
            split_attn(4)
            take_lo("v", 0, 0, 4, 4)
            maxima(0, 0)
            recip(0, 0)
            split_attn(5)
            take_lo("v", 1, 0, 5, 5)
            take_lo("v", 2, 0, 6, 6)
            for g in range(GROUPS):
                for n in range(8):
                    item = 8 * g + n
                    if item + 1 < 8 * GROUPS:
                        maxima(*divmod(item + 1, 8))
                    dve.wait_ge(pt_hi, item + 1)
                    dve.tensor_tensor(PTL[:, :, :].rearrange("p t n -> p (t n)"), PS[:, 2, :],
                                      PTH[:, :, :].bitcast(F32).rearrange("p t n -> p (t n)"),
                                      ALU.subtract).then_inc(pt_done, 1)
                    if item + 1 < 8 * GROUPS:
                        recip(*divmod(item + 1, 8))
                    ahead = parts(g, n)
                    for u in splits(g, n):
                        split_attn(u)
                    if ahead:
                        what, which = ahead[0]
                        take_lo(what, which + (0 if what == "v" else 2 * g), g + 1, part_count(g, n) + 1, 7)
                    if g == GROUPS - 1:
                        for c in OUT_TILES[n][0]:
                            out_residual(c)
                    dve.wait_ge(o_hi, item + 1)
                    for hh in range(2):
                        rows = slice(64 * hh, 64 * hh + 64)
                        cols = slice(P * (n % 4), P * (n % 4 + 1))
                        ins = dve.tensor_tensor(OL[rows, item_pair(g, n), cols], PSB[rows, 6, hh * P:(hh + 1) * P],
                                                OH[rows, item_pair(g, n), cols].bitcast(F32), ALU.subtract)
                    ins.then_inc(o_done, 1)
                    if g == GROUPS - 1:
                        for c in OUT_TILES[n][1]:
                            out_residual(c)
                    if len(ahead) > 1:
                        take_lo(ahead[1][0], ahead[1][1] + 2 * g, g + 1, part_count(g, n) + 2, 7)
            split_attn(U_MLP[1] - U_ATTN)
            for s in range(KT):
                dve.wait_ge(out_mm, KT + s + 1)
                residual(s % 4, s, 1, 16, LAT, by_column=True)
                if s:
                    sums(3, s - 1, LAT)
            sums(3, KT - 1, LAT)
            norm(3, LAT, (1, 24), lambda: split_attn(U_MLP[1] - U_ATTN + 1))
            mlp(1, "mlp1", LAT, 4)
            inverse_rms(4, 0, 0, LAT // P)
            dve.wait_ge(rec_done, norm_count(5))
            for n in (0, 2):
                t = OUT_ROWS[n]
                dve.wait_ge(turned, n + 1)
                for to, src in row_halves(t):
                    ins = dve.tensor_scalar(to, src, RMS[:, 1, t:t + 1], None, ALU.mult)
                ins.then_inc(row_done[0], 1)


_INS = ["x", "c", "ctx", "c_ctx", "norm1_g", "norm2_g", "ada_w", "ada_b", "conv_in_w", "conv_w", "conv_out_w",
        "attn_qkv_w", "attn_rpb", "attn_out_w", "mlp_w1", "mlp_w2", "final_g"]
_OUTS = [((1, 512, 1024), "float32")]


def kernel(**inputs):
    import numpy as _np
    import concourse.bacc as _bacc
    from concourse import mybir as _mybir
    from concourse.bass_utils import run_bass_kernel_spmd as _run

    nc = _bacc.Bacc("TRN2", target_bir_lowering=False, num_devices=1)
    arrays, args = {}, []
    for name in _INS:
        a = _np.ascontiguousarray(inputs[name])
        arrays[f"in_{name}_dram"] = a
        args.append(nc.dram_tensor(f"in_{name}_dram", a.shape, _mybir.dt.from_np(a.dtype), kind="ExternalInput").ap())
    arrays["consts_dram"] = constants()
    args.append(nc.dram_tensor("consts_dram", (P, NCONST + P), _mybir.dt.float32, kind="ExternalInput").ap())
    for i, (shape, dtype) in enumerate(_OUTS):
        dt = _mybir.dt.from_np(_np.dtype(dtype))
        args.append(nc.dram_tensor(f"out_{i}_dram", shape, dt, kind="ExternalOutput").ap())
    build(nc, *args)
    r = _run(nc, [arrays], core_ids=[0])
    return r.results[0]["out_0_dram"]
```
